# Optimizing a Trainium2 kernel written in Bass

```python
import jax
import jax.numpy as jnp
from jax import lax
import numpy as np

D_MODEL = 4096
BATCH = 1
SEQ = 256
DEPTH = 1

CTX_LEN = 256
GRID_W = 64
EPS = 1e-6

MLA_HEADS = 12
MLA_NOPE = 128
MLA_ROPE = 64
MLA_V = 128
MLA_Q_RANK = 1024
MLA_KV_RANK = 512
MLA_WIDTH = MLA_HEADS * MLA_V
MLA_SCALE = (MLA_NOPE + MLA_ROPE) ** -0.5
ROPE_BASE = 10000.0
Q_BLOCK = 128

ML_HEADS = 8
ML_DQK = 96
ML_DV = 192
ML_WIDTH = ML_HEADS * ML_DV
ML_CHUNK = 64

POOL_WINDOWS = (2, 4, 8, 16)
POOL_GROUPS = 4
POOL_GC = 256
POOL_WIDTH = POOL_GROUPS * POOL_GC

MIX_WIDTH = MLA_WIDTH + ML_WIDTH + POOL_WIDTH

IN_SIZES = (MLA_Q_RANK, MLA_KV_RANK, MLA_ROPE,
            ML_HEADS * ML_DQK, ML_HEADS * ML_DQK, ML_WIDTH, ML_WIDTH,
            2 * ML_HEADS, 2 * ML_HEADS, POOL_WIDTH, MIX_WIDTH)
IN_OFFSETS = tuple(int(v) for v in np.cumsum(IN_SIZES)[:-1])
N_IN = int(sum(IN_SIZES))

kernel_name = "hybrid_mla_mlstm_pool_dit"

def rms_norm(x, w):
    xf = x.astype(jnp.float32)
    y = xf * lax.rsqrt(jnp.mean(xf * xf, axis=-1, keepdims=True) + EPS)
    return (y * w.astype(jnp.float32)).astype(x.dtype)

def axial_rope(rows):
    row = jnp.repeat(jnp.arange(rows, dtype=jnp.float32), GRID_W)
    col = jnp.tile(jnp.arange(GRID_W, dtype=jnp.float32), rows)
    n_freq = MLA_ROPE // 4
    inv = jnp.power(ROPE_BASE, -jnp.arange(n_freq, dtype=jnp.float32) / n_freq)
    ang = jnp.concatenate([row[:, None] * inv, col[:, None] * inv], axis=-1)
    return jnp.cos(ang), jnp.sin(ang)

def apply_rope(x, cos, sin):
    xf = x.astype(jnp.float32)
    x1, x2 = jnp.split(xf, 2, axis=-1)
    return jnp.concatenate([x1 * cos - x2 * sin, x1 * sin + x2 * cos], axis=-1).astype(x.dtype)

def mla_project(cq, ckv, krope, q_norm_w, kv_norm_w, w_uq, w_ukv, rope):
    B, L, _ = cq.shape
    q = (rms_norm(cq, q_norm_w) @ w_uq).reshape(B, L, MLA_HEADS, MLA_NOPE + MLA_ROPE)
    kv = (rms_norm(ckv, kv_norm_w) @ w_ukv).reshape(B, L, MLA_HEADS, MLA_NOPE + MLA_V)
    q_nope, q_rope = q[..., :MLA_NOPE], q[..., MLA_NOPE:]
    k_nope, v = kv[..., :MLA_NOPE], kv[..., MLA_NOPE:]
    if rope is not None:
        cos, sin = rope
        q_rope = apply_rope(q_rope, cos[:, None], sin[:, None])
        krope = apply_rope(krope, cos, sin)
    k_rope = jnp.broadcast_to(krope[:, :, None, :], (B, L, MLA_HEADS, MLA_ROPE))
    q = jnp.concatenate([q_nope, q_rope], axis=-1)
    k = jnp.concatenate([k_nope, k_rope], axis=-1)
    return q, k, v

def attend(q, k, v):
    s = jnp.einsum("bqhd,bkhd->bhqk", q, k).astype(jnp.float32) * MLA_SCALE
    p = jax.nn.softmax(s, axis=-1).astype(v.dtype)
    return jnp.einsum("bhqk,bkhd->bqhd", p, v)

def blockwise_attention(q, k_all, v_all):
    B, S, H, Dk = q.shape
    nb = S // Q_BLOCK
    qb = jnp.moveaxis(q.reshape(B, nb, Q_BLOCK, H, Dk), 1, 0)
    out = lax.map(lambda qi: attend(qi, k_all, v_all), qb)
    return jnp.moveaxis(out, 0, 1).reshape(B, S, H * MLA_V)

def _to_chunks(a):
    B, L, H = a.shape[:3]
    a = a.reshape((B, L // ML_CHUNK, ML_CHUNK, H) + a.shape[3:])
    return jnp.moveaxis(a, (1, 3), (0, 2))

def mlstm_scan(q, k, v, li, lf, state, with_out):
    B, L, H, _ = q.shape
    causal = jnp.tril(jnp.ones((ML_CHUNK, ML_CHUNK), dtype=bool))

    def step(carry, xs):
        C, n, m = carry
        qc, kc, vc, lic, lfc = xs
        b = jnp.cumsum(lfc, axis=-1)
        b_end = b[..., -1]
        a = b_end[..., None] - b + lic
        m_new = jnp.maximum(b_end + m, jnp.max(a, axis=-1))
        decay = jnp.exp(b_end + m - m_new)
        w = jnp.exp(a - m_new[..., None])
        C_new = decay[..., None, None] * C + jnp.einsum("bht,bhtv,bhtk->bhvk", w, vc, kc)
        n_new = decay[..., None] * n + jnp.einsum("bht,bhtk->bhk", w, kc)
        if not with_out:
            return (C_new, n_new, m_new), None
        logw = jnp.where(causal, b[..., :, None] - b[..., None, :] + lic[..., None, :], -jnp.inf)
        m_t = jnp.maximum(b + m[..., None], jnp.max(logw, axis=-1))
        inter = jnp.exp(b + m[..., None] - m_t)
        s = jnp.einsum("bhtk,bhsk->bhts", qc, kc) * jnp.exp(logw - m_t[..., None])
        num = inter[..., None] * jnp.einsum("bhvk,bhtk->bhtv", C, qc) + jnp.einsum("bhts,bhsv->bhtv", s, vc)
        den = inter * jnp.einsum("bhk,bhtk->bht", n, qc) + jnp.sum(s, axis=-1)
        h = num / jnp.maximum(jnp.abs(den), jnp.exp(-m_t))[..., None]
        return (C_new, n_new, m_new), h

    xs = tuple(_to_chunks(a) for a in (q, k, v, li, lf))
    state, h = lax.scan(step, state, xs)
    if with_out:
        h = jnp.moveaxis(h, (0, 2), (1, 3)).reshape(B, L, H, ML_DV)
    return state, h

def mlstm_streams(mq, mk, mv, mi, mf, b_i, b_f):
    B, L, _ = mq.shape
    q = mq.astype(jnp.float32).reshape(B, L, ML_HEADS, ML_DQK)
    k = mk.astype(jnp.float32).reshape(B, L, ML_HEADS, ML_DQK) * (ML_DQK ** -0.5)
    v = mv.astype(jnp.float32).reshape(B, L, ML_HEADS, ML_DV)
    li = mi.astype(jnp.float32).reshape(B, L, 2, ML_HEADS) + b_i.astype(jnp.float32)
    lf = jax.nn.log_sigmoid(mf.astype(jnp.float32).reshape(B, L, 2, ML_HEADS) + b_f.astype(jnp.float32))
    return q, k, v, li, lf

def mlstm_direction(stream, d, state, with_out):
    q, k, v, li, lf = stream
    li, lf = li[:, :, d], lf[:, :, d]
    if d == 1:
        q, k, v, li, lf = (a[:, ::-1] for a in (q, k, v, li, lf))
    state, h = mlstm_scan(q, k, v, li, lf, state, with_out)
    if with_out and d == 1:
        h = h[:, ::-1]
    return state, h

def mlstm_out(h, o, norm_w):
    B, L = h.shape[:2]
    hn = h * lax.rsqrt(jnp.mean(h * h, axis=-1, keepdims=True) + EPS)
    hn = hn.reshape(B, L, ML_WIDTH) * norm_w.astype(jnp.float32)
    return (hn * jax.nn.sigmoid(o.astype(jnp.float32))).astype(o.dtype)

def mlstm_mixer(lat, ctx, b_i, b_f, norm_w, o_lat, o_ctx, ctx_out):
    lat_s = mlstm_streams(*lat, b_i, b_f)
    ctx_s = mlstm_streams(*ctx, b_i, b_f)
    B = lat_s[0].shape[0]
    zero = (jnp.zeros((B, ML_HEADS, ML_DV, ML_DQK), jnp.float32),
            jnp.zeros((B, ML_HEADS, ML_DQK), jnp.float32),
            jnp.zeros((B, ML_HEADS), jnp.float32))
    h_lat, h_ctx = [], []
    for d in (0, 1):
        st, hc = mlstm_direction(ctx_s, d, zero, ctx_out)
        _, hl = mlstm_direction(lat_s, d, st, True)
        h_lat.append(hl)
        h_ctx.append(hc)
    y_lat = mlstm_out(h_lat[0] + h_lat[1], o_lat, norm_w)
    y_ctx = mlstm_out(h_ctx[0] + h_ctx[1], o_ctx, norm_w) if ctx_out else None
    return y_lat, y_ctx

def pool_mix(u, pool_w, pool_scale):
    B, L, _ = u.shape
    uf = u.astype(jnp.float32).reshape(B, L, POOL_GROUPS, POOL_GC)
    csum = jnp.concatenate([jnp.zeros((B, 1, POOL_GROUPS, POOL_GC), jnp.float32),
                            jnp.cumsum(uf, axis=1)], axis=1)
    t = jnp.arange(L)
    groups = []
    for g, w in enumerate(POOL_WINDOWS):
        lo = jnp.clip(t - w // 2, 0, L)
        hi = jnp.clip(t + w - w // 2, 0, L)
        mean = (csum[:, hi, g] - csum[:, lo, g]) / (hi - lo).astype(jnp.float32)[None, :, None]
        groups.append(mean - uf[:, :, g])
    pooled = jnp.stack(groups, axis=2)
    y = jnp.einsum("blgc,gcd->blgd", pooled, pool_w.astype(jnp.float32)).reshape(B, L, POOL_WIDTH)
    return (y * pool_scale.astype(jnp.float32)).astype(u.dtype)

def mixer_layer(h, hc, rope, w_in, q_norm_w, kv_norm_w, w_uq, w_ukv, b_i, b_f, ml_norm_w,
                pool_w, pool_scale, w_out, ctx_out):
    B, S, _ = h.shape
    cq, ckv, kr, mq, mk, mv, mo, mi, mf, pu, z = jnp.split(h @ w_in, IN_OFFSETS, axis=-1)
    cq_c, ckv_c, kr_c, mq_c, mk_c, mv_c, mo_c, mi_c, mf_c, pu_c, z_c = jnp.split(hc @ w_in, IN_OFFSETS, axis=-1)
    q_l, k_l, v_l = mla_project(cq, ckv, kr, q_norm_w, kv_norm_w, w_uq, w_ukv, rope)
    q_c, k_c, v_c = mla_project(cq_c, ckv_c, kr_c, q_norm_w, kv_norm_w, w_uq, w_ukv, None)
    k_all = jnp.concatenate([k_c, k_l], axis=1)
    v_all = jnp.concatenate([v_c, v_l], axis=1)
    a_lat = blockwise_attention(q_l, k_all, v_all)
    ml_lat, ml_ctx = mlstm_mixer((mq, mk, mv, mi, mf), (mq_c, mk_c, mv_c, mi_c, mf_c),
                                 b_i, b_f, ml_norm_w, mo, mo_c, ctx_out)
    p_lat = pool_mix(pu, pool_w, pool_scale)
    y = (jnp.concatenate([a_lat, ml_lat, p_lat], axis=-1) * jax.nn.silu(z)) @ w_out
    if not ctx_out:
        return y, None
    a_ctx = attend(q_c, k_c, v_c).reshape(B, hc.shape[1], MLA_WIDTH)
    p_ctx = pool_mix(pu_c, pool_w, pool_scale)
    yc = (jnp.concatenate([a_ctx, ml_ctx, p_ctx], axis=-1) * jax.nn.silu(z_c)) @ w_out
    return y, yc

def setup_inputs(seed: int = 0) -> dict:
    key = jax.random.key(seed)
    ks = jax.random.split(key, 19)
    D = D_MODEL

    def nrm(k, shape, s):
        return jax.random.normal(k, shape, jnp.float32) * s

    return {
        "x": nrm(ks[0], (BATCH, SEQ, D), 1.0),
        "c": nrm(ks[1], (BATCH, D), 1.0),
        "ctx": nrm(ks[2], (BATCH, CTX_LEN, D), 1.0),
        "c_ctx": nrm(ks[3], (D,), 1.0),
        "norm_w": 1.0 + nrm(ks[4], (DEPTH, D), 0.05),
        "w_mod": nrm(ks[5], (DEPTH, D, 3 * D), 0.5 * D ** -0.5),
        "b_mod": nrm(ks[6], (DEPTH, 3 * D), 0.02),
        "w_in": nrm(ks[7], (DEPTH, D, N_IN), D ** -0.5),
        "q_norm_w": 1.0 + nrm(ks[8], (DEPTH, MLA_Q_RANK), 0.05),
        "kv_norm_w": 1.0 + nrm(ks[9], (DEPTH, MLA_KV_RANK), 0.05),
        "w_uq": nrm(ks[10], (DEPTH, MLA_Q_RANK, MLA_HEADS * (MLA_NOPE + MLA_ROPE)), MLA_Q_RANK ** -0.5),
        "w_ukv": nrm(ks[11], (DEPTH, MLA_KV_RANK, MLA_HEADS * (MLA_NOPE + MLA_V)), MLA_KV_RANK ** -0.5),
        "ml_b_i": nrm(ks[12], (DEPTH, 2, ML_HEADS), 0.1),
        "ml_b_f": jnp.linspace(3.0, 6.0, ML_HEADS, dtype=jnp.float32) + nrm(ks[13], (DEPTH, 2, ML_HEADS), 0.1),
        "ml_norm_w": 1.0 + nrm(ks[14], (DEPTH, ML_WIDTH), 0.05),
        "pool_w": nrm(ks[15], (DEPTH, POOL_GROUPS, POOL_GC, POOL_GC), POOL_GC ** -0.5),
        "pool_scale": 1.0 + nrm(ks[16], (DEPTH, POOL_WIDTH), 0.05),
        "w_out": nrm(ks[17], (DEPTH, MIX_WIDTH, D), MIX_WIDTH ** -0.5),
        "final_norm_w": 1.0 + nrm(ks[18], (D,), 0.05),
    }

def reference(x, c, ctx, c_ctx, norm_w, w_mod, b_mod, w_in, q_norm_w, kv_norm_w, w_uq, w_ukv,
              ml_b_i, ml_b_f, ml_norm_w, pool_w, pool_scale, w_out, final_norm_w):
    B, S, _ = x.shape
    ROWS = S // GRID_W
    rope = axial_rope(ROWS)
    for l in range(DEPTH):
        ctx_out = l < DEPTH - 1
        mod = jax.nn.silu(c) @ w_mod[l] + b_mod[l]
        mod_c = jax.nn.silu(c_ctx) @ w_mod[l] + b_mod[l]
        shift, scale, gate = jnp.split(mod, 3, axis=-1)
        shift_c, scale_c, gate_c = jnp.split(mod_c, 3, axis=-1)
        h = rms_norm(x, norm_w[l]) * (1.0 + scale[:, None]) + shift[:, None]
        hc = rms_norm(ctx, norm_w[l]) * (1.0 + scale_c) + shift_c
        y, yc = mixer_layer(h, hc, rope, w_in[l], q_norm_w[l], kv_norm_w[l], w_uq[l], w_ukv[l],
                            ml_b_i[l], ml_b_f[l], ml_norm_w[l], pool_w[l], pool_scale[l], w_out[l], ctx_out)
        x = x + gate[:, None] * y
        if ctx_out:
            ctx = ctx + gate_c * yc
    return rms_norm(x, final_norm_w)


_drawn_inputs = setup_inputs


def setup_inputs(seed=0):
    import zlib

    import numpy as np

    out = dict(_drawn_inputs(seed))
    spreads = {}
    factors = {'norm_w': 5.162,
     'b_mod': 5.139,
     'q_norm_w': 8.0,
     'kv_norm_w': 8.0,
     'w_uq': 6.1,
     'ml_b_i': 64.0,
     'ml_norm_w': 55.576,
     'pool_scale': 8.0}
    for name, (base, spread) in spreads.items():
        noise = np.random.default_rng([zlib.crc32(name.encode()), seed]).standard_normal(out[name].shape)
        drawn = base * np.exp(spread * noise) if base else spread * noise
        out[name] = jnp.asarray(drawn.astype(out[name].dtype))
    for name, factor in factors.items():
        out[name] = (out[name] * factor).astype(out[name].dtype)
    return out
```

```python
from contextlib import ExitStack

import numpy as np
import concourse.bass as bass
from concourse import mybir

F32 = mybir.dt.float32
F32R = mybir.dt.float32r
ALU = mybir.AluOpType
ACT = mybir.ActivationFunctionType
AX_X = mybir.AxisListType.X

P = 128
D = 4096
S = 256
TT = 4
EPS = 1e-6
GRID_W = 64
ROPE_BASE = 10000.0

HEADS, NOPE, ROPE, DV = 12, 128, 64, 128
PAIRS = HEADS // 2
Q_RANK, KV_RANK = 1024, 512
MLA_SCALE = (NOPE + ROPE) ** -0.5
MLH, DQK, MLV = 8, 96, 192
ML_SCALE = DQK ** -0.5
WINDOWS, PC = (2, 4, 8, 16), 256
AT_ML, AT_POOL = HEADS * DV, HEADS * DV + MLH * MLV

W = 512
KT = 4
NG = D // (KT * P)
RAW = 4
PART = 4
PAIR_BANKS = 3
MOD_BANK, TR_BANK = 6, 7

C_CQ, C_CKV, C_KR, C_MQ, C_MK, C_MV, C_MO, C_GATES, C_PU, C_Z = (
    0, 1024, 1536, 1600, 2368, 3136, 4672, 6208, 6240, 7264)

KEPT = {"z": (2, 4096), "mv": (4, 1536), "mk": (4, 768), "mo": (2, 1536), "mq": (2, 768), "pu": (2, 1024),
        "cq": (2, 1024), "ckv": (4, 512), "kg": (4, 96)}


def places():
    at, out = 0, {}
    for name, (t, w) in KEPT.items():
        out[name] = at
        at += t * w
    return out, at


KEPT_AT, KEPT_SIZE = places()


def in_tiles():
    both = [("ckv", 0, C_CKV, W)]
    both += [("mk", c, C_MK + c, 384) for c in (0, 384)]
    both += [("mv", c, C_MV + c, W) for c in (0, 512, 1024)]
    both += [("kg", 0, C_KR, 96)]
    latent = [("cq", c, C_CQ + c, W) for c in (0, 512)] + [("mq", c, C_MQ + c, 384) for c in (0, 384)]
    latent += [("mo", c, C_MO + c, W) for c in (0, 512, 1024)] + [("pu", c, C_PU + c, W) for c in (0, 512)]
    latent += [("z", c, C_Z + c, W) for c in range(0, D, W)]
    tiles = []
    for i, tile in enumerate(both):
        tiles.append(tile)
        n = len(latent) * (i + 1) // len(both) - len(latent) * i // len(both)
        done = len(tiles) - i - 1
        tiles += latent[done:done + n]
    return tiles


SHIFT, SCALE, GATE = range(3)


class Product:

    def __init__(self, tiles, mods, last_mods, ring, raw0, chunk0, pair0, tr0, hT0, mod0, turn_at):
        self.tiles, self.n, self.ring = tiles, len(tiles), ring
        self.order = (self.place(mods), self.place(last_mods))
        self.pair = []
        at = 0
        for name, *_ in tiles:
            k = KEPT[name][0] // 2 if name in KEPT else 1
            self.pair.append((at, k))
            at += k
        self.npairs, self.nraw, self.nmods = at, len(self.order[0]), len(mods)
        self.ntr = 4 + len(mods) // 8
        self.raw0, self.chunk0, self.pair0, self.tr0, self.hT0, self.mod0 = raw0, chunk0, pair0, tr0, hT0, mod0
        self.turn_at = turn_at

    def place(self, mods):
        out, left = [], list(mods)
        for j in range(self.n):
            if j == self.n - 1:
                out += left
                left = []
            out.append(("w", j))
            if left:
                out.append(left.pop(0))
        return out

    def slot(self, idx):
        return (self.raw0 + idx) % self.ring

    def landed_at(self, idx, g):
        return g * (16 * (self.nraw // self.ring)) + 16 * ((self.raw0 + idx) // self.ring + 1)

    def chunk(self, j, k, g):
        return g * (KT * self.n) + (self.chunk0 + KT * j + k + 1)

    def pair_free(self, q, g, first):
        last = q - PAIR_BANKS
        if q < PAIR_BANKS:
            if first:
                return None
            last = max(i for i in range(self.npairs) if i % PAIR_BANKS == q % PAIR_BANKS) - self.npairs
        return g * self.npairs + (self.pair0 + last + 1)

    def free(self, idx, g, first):
        back = idx - self.ring
        order = self.order[0]
        if back < 0:
            if first:
                return None
            back, g = back + self.nraw, g - 1
        elif isinstance(g, int) and g == NG - 1:
            order = self.order[1]
        kind = order[back]
        if kind[0] == "w":
            return True, self.chunk(kind[1], KT - 1, g)
        return False, g * self.nmods + (self.mod0 + sum(1 for o in order[:back + 1] if o[0] == "m"))


MODS = [("m", kind, kc) for kind in (SHIFT, SCALE, GATE) for kc in range(8)]
PRO_MODS = 16
PRO_TR = 2 + 2 + 4
IN = Product(in_tiles(), MODS, MODS[16:], ring=RAW, raw0=PRO_MODS, chunk0=0, pair0=0, tr0=PRO_TR, hT0=4,
             mod0=PRO_MODS, turn_at=18)
IN_RAW = PRO_MODS + IN.nraw * (NG - 1) + len(IN.order[1])
IN_CHUNKS = KT * IN.n * NG
IN_PAIRS = IN.npairs * NG
IN_TR = PRO_TR + IN.ntr * (NG - 1) + 1
IN_VECS = 2 + 3 * (NG - 1) + 1
MLA_CHUNKS = 12
OUT = Product([("y", n * W, n * W, W) for n in range(D // W)], [], [], ring=RAW, raw0=2,
              chunk0=IN_CHUNKS + MLA_CHUNKS * PAIRS, pair0=IN_PAIRS, tr0=IN_TR + 4, hT0=4 * NG + 4, mod0=0, turn_at=2)
assert IN_RAW % RAW == 0 and IN.nraw % RAW == 0 and OUT.nraw % OUT.ring == 0 and IN.n * KT % PART == 0
PARAM_LOADS = 3 + 6 + 4
G_STEPS = 12


def turn_events(pr, last):
    pe, copies, others = {}, {}, {}
    use = 0

    def at(j, what, number):
        nonlocal use
        pe.setdefault(j, []).append((what, number, use))
        others.setdefault(j + 1, []).append((what, number, use))
        use += 1

    if pr.nmods and not last:
        copies[8] = copies[16] = copies[pr.n - 1] = True
        at(8, "vec", SHIFT)
        at(16, "vec", SCALE)
    if pr.nmods and last:
        copies[8] = True
        at(8, "vec", GATE)
    if not last:
        for k in range(KT):
            at(pr.turn_at + k, "turn", k)
        if pr.nmods:
            at(pr.n - 1, "vec", GATE)
    return pe, copies, others


def hybrid_kernel(nc, x, c, ctx, c_ctx, norm_w, w_mod, b_mod, w_in, q_norm_w, kv_norm_w, w_uq, w_ukv, ml_b_i,
                  ml_b_f, ml_norm_w, pool_w, pool_scale, w_out, final_norm_w, tables, masks, bands, out):
    with ExitStack() as stack:
        def sb(name, shape, dt=F32):
            return stack.enter_context(nc.sbuf_tensor(name, shape, dt))

        def sem(name):
            return stack.enter_context(nc.semaphore(name))

        kept = sb("kept", [P, KEPT_SIZE])
        raw = sb("raw", [P, RAW, KT, W])
        part = sb("part", [P, PART, 2, W], F32R)
        hT = sb("hT", [P, 2, 2, KT, TT * P], F32R)
        xs = sb("xs", [P, TT, KT * P])
        modsb = sb("modsb", [P, W])
        hf = sb("hf", [P, W])
        tab = sb("tab", [P, 258])
        cT = sb("cT", [P, 2, 32])
        par1 = sb("par1", [P, P])
        par2 = sb("par2", [P, 96])
        colsc = sb("colsc", [P, 32])
        shiftv = sb("shiftv", [P, KT, 2])
        scalet = sb("scalet", [P, KT, 2])
        scalev = sb("scalev", [P, KT, 2])
        gateK = sb("gateK", [P, 32])
        sums = sb("sums", [P, 8])
        rstd = sb("rstd", [P, 8])
        epst = sb("epst", [P, 2])
        bif = sb("bif", [MLH, 4])
        negm = sb("negm", [P, 4])
        rows_s = sb("rows_s", [P, 4])
        rinv = sb("rinv", [P, 4])
        Gt = sb("Gt", [P, 8, MLH])
        Et = sb("Et", [P, 4, MLH])
        Gh = sb("Gh", [P, 8])
        Eh = sb("Eh", [P, 4])
        den = sb("den", [P, 4])
        dent = sb("dent", [P, 4])
        selh = sb("selh", [MLH, P])
        ssh = sb("ssh", [P, 2])
        ssall = sb("ssall", [P, MLH, 2])
        rall = sb("rall", [P, MLH, 2])

        ident = tab[:, 0:128]
        cosv = tab[:, 128:192].rearrange("p (t f) -> p t f", t=2)
        sinv = tab[:, 192:256].rearrange("p (t f) -> p t f", t=2)
        sel2 = tab[:, 256:258]
        par_rows = hf[:, 0:256].rearrange("p (a c) -> p a c", a=2)

        def keep(name):
            t, w = KEPT[name]
            return kept[:, KEPT_AT[name]:KEPT_AT[name] + t * w].rearrange("p (t c) -> p t c", t=t)

        kv = {name: keep(name) for name in KEPT}
        xfull = kept[:, 0:4 * D].rearrange("p (t c) -> p t c", t=4)

        def arena(base, spec):
            views, at = {}, 0
            for name, shape in spec.items():
                size = int(np.prod(shape))
                v = base[:, at:at + size]
                if len(shape) == 2:
                    v = v.rearrange("p (a b) -> p a b", a=shape[0])
                elif len(shape) == 3:
                    v = v.rearrange("p (a b c) -> p a b c", a=shape[0], b=shape[1])
                views[name] = v
                at += size
            return views

        free16 = kept[:, KEPT_AT["cq"]:KEPT_AT["cq"] + 4096]
        free8 = xs[:].rearrange("p t c -> p (t c)")
        A = arena(free16, {"knT": (2, 512), "v": (4, 256), "qnT": (2, 256), "qrT": (256,), "krT": (512,),
                           "qr": (2, 2, 64), "ra": (2, 2, 32)})
        key2 = hf[:].rearrange("p (t e c) -> p t e c", t=TT, e=2)
        prob = free8.rearrange("p (i k) -> p i k", i=4)
        probT = (modsb, hf)
        L = arena(free16, {"kst": (4, 96), "qst": (2, 96), "kT": (512,), "qT": (256,), "vst": (4, 194), "vst_odd": (4, 194), "H": (2, 192),
                           "negM": (2, 256), "mask": (2, P)})
        R = arena(free16, {"G": (2, 512), "M": (2, 512)})
        R2 = arena(free8, {"li": (2, 512), "lf": (2, 512)})
        wts = [flat.rearrange("p (d s t) -> p d s t", d=2, s=4) for flat in (free8, raw[:, 3].rearrange("p k c -> p (k c)"))]
        vst = [L["vst"], L["vst_odd"]]
        band = raw[:, 0].rearrange("p k c -> p (k c)").rearrange("p (s g t) -> p s g t", s=2, g=4)
        poolw = raw[:, 1].rearrange("p k c -> p (k c)").rearrange("p (g c d) -> p g c d", g=4, c=2)
        gateR = free8[0:32, 0:P]
        poolT = free8.rearrange("p (i t) -> p i t", i=8)
        psum = stack.enter_context(nc.psum_tensor("psum", [P, 8, W], F32))
        TR, MOD = psum[:, TR_BANK, :], psum[:, MOD_BANK, :]

        def place_of(name, col, width, pair, pr):
            if pr is IN:
                return kv[name][:, 2 * pair:2 * pair + 2, col:col + width]
            base = KEPT_AT["mv"] + col * 2
            return kept[:, base:base + 2 * width].rearrange("p (t c) -> p t c", t=2)

        def banks(q):
            return 2 * (q % PAIR_BANKS)

        gates_landed = sem("gates_landed")
        par_in, x_in, xs_in = sem("par_in"), sem("x_in"), sem("xs_in")
        landed = {IN: [sem(f"landed{i}") for i in range(RAW)], OUT: [sem(f"out_landed{i}") for i in range(RAW)]}
        eps_set, par_turned, par_ready, c_ready = sem("eps_set"), sem("par_turned"), sem("par_ready"), sem("c_ready")
        sq_done, rms_root, rstd_ready = sem("sq_done"), sem("rms_root"), sem("rstd_ready")
        mod_zero = sem("mod_zero")
        xs_ready = sem("xs_ready")
        hi_done, lo_done, chunk_used = sem("hi_done"), sem("lo_done"), sem("chunk_used")
        mod_used, mod_copied = sem("mod_used"), sem("mod_copied")
        tr_filled, tr_read, vec_ready, scale_tmp = sem("tr_filled"), sem("tr_read"), sem("vec_ready"), sem("scale_tmp")
        hiT_done, full_done, loT_done = sem("hiT_done"), sem("full_done"), sem("loT_done")
        added = sem("added")
        cq_sq, cq_root, cq_rstd, cq_scaled = sem("cq_sq"), sem("cq_root"), sem("cq_rstd"), sem("cq_scaled")
        lat_turned, lat_hi, lat_full, lat_lo = sem("lat_turned"), sem("lat_hi"), sem("lat_full"), sem("lat_lo")
        silu_done, kr_tmp, kr_roped, kr_turned, krT_ready = (
            sem("silu_done"), sem("kr_tmp"), sem("kr_roped"), sem("kr_turned"), sem("krT_ready"))
        q_tmp, q_roped, qr_turned = sem("q_tmp"), sem("q_roped"), sem("qr_turned")
        qn_copied, qrT_copied, kn_copied, v_copied = sem("qn_copied"), sem("qrT_copied"), sem("kn_copied"), sem("v_copied")
        s_filled, max_done, negm_ready, p_ready = sem("s_filled"), sem("max_done"), sem("negm_ready"), sem("p_ready")
        p_turned, pT_ready, o_filled, rinv_ready, o_stored = (
            sem("p_turned"), sem("pT_ready"), sem("o_filled"), sem("rinv_ready"), sem("o_stored"))
        g_turned, g_step, gabs, g_exp, g_ln, em_in = (
            sem("g_turned"), sem("g_step"), sem("gabs"), sem("g_exp"), sem("g_ln"), sem("em_in"))
        gt_turned, gt_ready, et_ready, mask_in = sem("gt_turned"), sem("gt_ready"), sem("et_ready"), sem("mask_in")
        staged, picked, e_picked, ml_turned, ml_copied, sT_filled = (
            sem("staged"), sem("picked"), sem("e_picked"), sem("ml_turned"), sem("ml_copied"), sem("sT_filled"))
        arg_done, w_exp, w_mul, w_ready, h_filled = (
            sem("arg_done"), sem("w_exp"), sem("w_mul"), sem("w_ready"), sem("h_filled"))
        h_step, h_ready, h_sq, h_kept, ml_root, ml_rstd, ml_mixed = (
            sem("h_step"), sem("h_ready"), sem("h_sq"), sem("h_kept"), sem("ml_root"), sem("ml_rstd"), sem("ml_mixed"))
        pooled, pooled_copied, pool_filled, pool_mixed = (
            sem("pooled"), sem("pooled_copied"), sem("pool_filled"), sem("pool_mixed"))
        gate_turned, gate_row, gate_filled = sem("gate_turned"), sem("gate_row"), sem("gate_filled")
        xe_in, fw_in, e_step, e_sq, e_root, e_rstd, e_out, out_done = (
            sem("xe_in"), sem("fw_in"), sem("e_step"), sem("e_sq"), sem("e_root"), sem("e_rstd"), sem("e_out"),
            sem("out_done"))

        block = stack.enter_context(nc.Block())

        def groups(engine, pr, run):
            run(pr, 0, 0, True, False)
            with engine.Fori(0, (NG - 2) // 2) as it:
                run(pr, it * 2 + 1, 1, False, False)
                run(pr, it * 2 + 2, 0, False, False)
            run(pr, NG - 1, 1, False, True)

        def heads(engine, step, peeled):
            step(0, 0)
            with engine.Fori(0, (MLH - 2 - peeled) // 2) as it:
                step(it * 2 + 1, 1)
                step(it * 2 + 2, 0)
            for h in range(MLH - 1 - peeled, MLH - 1):
                step(h, h % 2)

        @block.sync
        def _(sp):
            def load_mod(slot, kind, kc, g):
                src = w_mod[0, kc * KT * P:(kc + 1) * KT * P, bass.ds(g * W + kind * D, W)]
                sp.dma_start(raw[:, slot], src.rearrange("(k p) n -> p k n", p=P)).then_inc(landed[IN][slot], 16)

            def load_xs(g):
                for n, t in enumerate((x[0], ctx[0])):
                    src = t[:, bass.ds(g * W, W)].rearrange("(t p) n -> p t n", p=P)
                    sp.dma_start(xs[:, 2 * n:2 * n + 2, :], src).then_inc(xs_in, 16)

            def alone(pr, idx, last):
                if pr is not IN or not 0 < idx < len(pr.order[last]):
                    return False
                item = pr.order[last][idx]
                if item[0] == "w" and pr.tiles[item[1]][2] == 0:
                    assert idx == 2
                    return True
                return False

            def group(pr, g, buf, first, last):
                weight = w_in[0] if pr is IN else w_out[0]
                for idx, item in enumerate(pr.order[last]):
                    if pr is IN and idx == 6 and not last:
                        sp.wait_ge(tr_filled, g * pr.ntr + pr.tr0)
                        load_xs(g + 1)
                    slot = pr.slot(idx)
                    if pr is OUT and first and idx == 1:
                        sp.wait_ge(h_kept, MLH + 1)
                    if pr is OUT and first and idx == 2:
                        sp.wait_ge(pool_mixed, 8)
                    if pr is IN and first and idx < RAW:
                        sp.wait_ge(mod_used, PRO_MODS + idx - RAW + 1)
                    else:
                        if not alone(pr, idx, last) or first:
                            early = alone(pr, idx + 1, last) and not first
                            split, count = pr.free(idx + early, g, first) or (None, None)
                            assert not early or pr.free(idx, g, first)[0] == split
                            if split is not None:
                                sp.wait_ge(lo_done if split else mod_used, count)
                    if item[0] == "m":
                        load_mod(slot, item[1], item[2], g if item[1] == GATE else g + 1)
                        continue
                    name, _, col, width = pr.tiles[item[1]]
                    rows = weight[bass.ds(g * W, W), :]
                    dst = raw[:, slot, :, 0:width]
                    if name == "kg":
                        for at, n, col, there in ((0, 64, C_KR, landed[pr][slot]), (64, 32, C_GATES, gates_landed)):
                            src = rows[:, col:col + n].rearrange("(k p) n -> p k n", p=P)
                            sp.dma_start(dst[:, :, at:at + n], src).then_inc(there, 16)
                    else:
                        src = rows[:, col:col + width].rearrange("(k p) n -> p k n", p=P)
                        sp.dma_start(dst, src).then_inc(landed[pr][slot], 16)

            for kind in (SHIFT, SCALE):
                for kc in range(8):
                    n = 8 * kind + kc
                    if n >= RAW:
                        sp.wait_ge(mod_used, n - RAW + 1)
                    load_mod(n % RAW, kind, kc, 0)
                    if n == RAW - 1:
                        load_xs(0)
            groups(sp, IN, group)

            with sp.Fori(0, PAIRS) as hp:
                for t in range(3):
                    sp.wait_ge(lo_done, hp * MLA_CHUNKS + (IN_CHUNKS - MLA_CHUNKS + KT * (t + 1)))
                    if t < 2:
                        src = w_uq[0, t * W:(t + 1) * W, bass.ds(hp * 384, 384)]
                        dst = raw[:, t, :, 0:384]
                    else:
                        src = w_ukv[0, :, bass.ds(hp * 512, 512)]
                        dst = raw[:, t]
                    sp.dma_start(dst, src.rearrange("(k p) n -> p k n", p=P)).then_inc(landed[IN][t], 16)

            sp.wait_ge(o_stored, 4 * PAIRS + 1)
            sp.dma_start(L["mask"], masks.rearrange("p (d t) -> p d t", d=2)).then_inc(mask_in, 16)
            sp.wait_ge(lo_done, OUT.chunk0)
            sp.dma_start(raw[:, 0].rearrange("p k c -> p (k c)"), bands).then_inc(landed[OUT][0], 16)
            src = pool_w[0].rearrange("g (c p) d -> p (g c) d", p=P)
            sp.dma_start(raw[:, 1].rearrange("p k (b c) -> p (k b) c", b=2), src).then_inc(landed[OUT][1], 16)
            groups(sp, OUT, group)

            sp.wait_ge(tr_filled, OUT.tr0 + OUT.ntr * (NG - 1))
            sp.wait_ge(lo_done, OUT.chunk0 + KT * OUT.n * NG)
            for t in range(2):
                sp.dma_start(kv["z"][:, t, :], x[0, t * P:(t + 1) * P, :]).then_inc(xe_in, 16)
            sp.dma_start(free16[:, 0:4096], final_norm_w.rearrange("(a n) -> a n", a=1).to_broadcast([P, D])).then_inc(fw_in, 16)
            for t in range(2):
                for n in range(0, OUT.n, 4):
                    sp.wait_ge(e_out, t * 8 + n + 4)
                    src = kept[:, KEPT_AT["mv"] + n * 2 * W:KEPT_AT["mv"] + (n + 4) * 2 * W]
                    src = src.rearrange("p (n t c) -> p n t c", n=4, t=2)[:, :, t, :]
                    dst = out[0, t * P:(t + 1) * P, n * W:(n + 4) * W].rearrange("p (n c) -> p n c", n=4)
                    sp.dma_start(dst, src).then_inc(out_done, 16)
            sp.wait_ge(out_done, 16 * 4)

        @block.gpsimd
        def _(pool):
            def scale_xs(g):
                pool.wait_ge(xs_in, g * 32 + 32)
                for t in range(TT):
                    nc.gpsimd.tensor_tensor(xs[:, t, :], xs[:, t, :], rstd[:, t:t + 1].to_broadcast([P, W]),
                                            ALU.mult).then_inc(xs_ready, 1)

            def stage_mix(g):
                if not isinstance(g, int) or g > 0:
                    pool.wait_ge(tr_filled, g * OUT.ntr + IN_TR)
                nc.gpsimd.tensor_copy(xs[:, 0:2, :], kv["z"][:, :, bass.ds(g * W, W)]).then_inc(xs_ready, 1)

            pool.wait_ge(rstd_ready, 1)
            scale_xs(0)
            with pool.Fori(1, NG) as g:
                scale_xs(g)

            pool.wait_ge(et_ready, 1)
            for v in vst:
                nc.gpsimd.memset(v[:, :, MLV:MLV + 1], 1.0).then_inc(staged, 1)
            pool.wait_ge(staged, 2)

            def stage_head(h):
                pool.wait_ge(ml_turned, h + 1)
                nc.gpsimd.tensor_copy(L["kst"], kv["mk"][:, :, bass.ds(h * DQK, DQK)]).then_inc(staged, 1)
                nc.gpsimd.tensor_copy(L["qst"], kv["mq"][:, :, bass.ds(h * DQK, DQK)]).then_inc(staged, 1)

            def strike(h, par):
                for d in range(2):
                    pool.wait_ge(w_mul, h * 2 + d + 2)
                    w = wts[par][:, d, 2:4, :].rearrange("p s (a c) -> p (s a) c", a=2)[:, ::3, :]
                    nc.gpsimd.tensor_tensor(w, w, L["mask"][:, d:d + 1].to_broadcast([P, 2, P]), ALU.mult).then_inc(w_ready, 1)

            def head_step(h, par):
                stage_head(h + 1)
                strike(h, par)

            stage_head(0)
            pool.wait_ge(mask_in, 16)
            heads(pool, head_step, 0)
            strike(MLH - 1, 1)
            pool.wait_ge(pool_filled, 8)
            pool.wait_ge(o_stored, 4 * PAIRS + 1)
            stage_mix(0)
            with pool.Fori(1, AT_ML // W) as g:
                stage_mix(g)
            pool.wait_ge(ml_mixed, 2 * MLH)
            pool.wait_ge(pool_mixed, 8)
            with pool.Fori(AT_ML // W, NG) as g:
                stage_mix(g)

        @block.scalar
        def _(act):
            for s in (p_ready, h_sq):
                act.sem_inc(s, 1)
            act.dma_start(tab[:], tables).then_inc(par_in, 16)
            act.dma_start(par_rows[0:96, 0], b_mod[0].rearrange("(a n) -> a n", n=P)).then_inc(par_in, 16)
            act.dma_start(par_rows[96:128, 0], norm_w[0].rearrange("(a n) -> a n", n=P)).then_inc(par_in, 16)
            rows = 0
            for src in (c[0], c_ctx, q_norm_w[0], kv_norm_w[0], ml_norm_w[0], pool_scale[0]):
                n = src.shape[0] // P
                act.dma_start(par_rows[rows:rows + n, 1], src.rearrange("(a n) -> a n", n=P)).then_inc(par_in, 16)
                rows += n
            for n, src in enumerate((ml_b_i[0, 0], ml_b_i[0, 1], ml_b_f[0, 0], ml_b_f[0, 1])):
                act.dma_start(bif[:, n:n + 1], src.rearrange("(h o) -> h o", o=1)).then_inc(par_in, 16)
            for t in range(TT):
                src = (x, ctx)[t // 2][0, (t % 2) * P:(t % 2 + 1) * P, :]
                act.dma_start(xfull[:, t, :], src).then_inc(x_in, 16)
            act.wait_ge(par_ready, 2)
            nc.scalar.activation(cT[:].rearrange("p a k -> p (a k)"), par2[:, 0:64], ACT.Silu).then_inc(c_ready, 1)
            act.wait_ge(x_in, 16 * TT)
            for t in range(TT):
                nc.scalar.activation(xfull[:, t, :], xfull[:, t, :], ACT.Square,
                                     accum_out=sums[:, t:t + 1]).then_inc(sq_done, 1)
            act.wait_ge(eps_set, 2)
            act.wait_ge(sq_done, TT)
            nc.scalar.activation(rstd[:, 0:4], sums[:, 0:4], ACT.Sqrt, bias=epst[:, 0:1], scale=1.0 / D).then_inc(rms_root, 1)

            def copy_mod(n, before):
                act.wait_ge(tr_filled, before)
                act.wait_ge(mod_used, n * 8 + 8)
                nc.scalar.copy(modsb[:], MOD).then_inc(mod_copied, 1)

            def turn(pr, g, buf, k, use, vecs):
                act.wait_ge(tr_filled, use + 1)
                if k == 0:
                    act.wait_ge(vec_ready, vecs)
                for i in range(2 if pr is IN else 1):
                    seg = slice(i * S, (i + 1) * S)
                    dst = hT[:, buf, 0, k, seg]
                    if pr is IN:
                        a = nc.scalar.activation(dst, TR[:, seg], ACT.Identity, bias=shiftv[:, k, i:i + 1],
                                                 scale=scalev[:, k, i:i + 1])
                    else:
                        a = nc.scalar.activation(dst, TR[:, seg], ACT.Copy, scale=scalev[:, k, 0:1])
                a.then_inc(hiT_done, 1)

            def split(pr, slot, j, k, g, width):
                place = (KT * j + k) % PART
                if pr is not IN or not (isinstance(g, int) and g == 0 and KT * j + k < PART):
                    act.wait_ge(chunk_used, pr.chunk(j, k, g) - PART)
                nc.scalar.copy(part[:, place, 0, 0:width], raw[:, slot, k, 0:width]).then_inc(hi_done, 1)

            def group(pr, g, buf, first, last):
                _, copies, others = turn_events(pr, last)
                for idx, item in enumerate(pr.order[last]):
                    if item[0] == "m":
                        continue
                    j = item[1]
                    slot = pr.slot(idx)
                    act.wait_ge(landed[pr][slot], pr.landed_at(idx, g))
                    if pr.tiles[j][0] == "kg":
                        act.wait_ge(gates_landed, g * 16 + 16)
                    for k in range(KT):
                        split(pr, slot, j, k, g, pr.tiles[j][3])
                    if j in copies:
                        kind = 0 if last else {8: 0, 16: 1, pr.n - 1: 2}[j]
                        copy_mod(g * 3 + (2 + kind), g * pr.ntr + (pr.tr0 + kind))
                    for what, number, use in others.get(j, ()):
                        if what == "turn":
                            vecs = g * 3 + 4 if pr is IN else g + (IN_VECS + 2)
                            turn(pr, g + 1, 1 - buf, number, g * pr.ntr + (pr.tr0 + use), vecs)

            copy_mod(0, 2)
            copy_mod(1, 3)
            for k in range(KT):
                turn(IN, 0, 0, k, 4 + k, 2)
            groups(act, IN, group)

            act.wait_ge(added, IN_PAIRS)
            for t in range(2):
                nc.scalar.activation(psum[:, 0:2, :], kv["cq"][:, t, :].rearrange("p (a c) -> p a c", a=2), ACT.Square,
                                     accum_out=sums[:, t:t + 1]).then_inc(cq_sq, 1)
                act.wait_ge(cq_sq, t + 1)
            for t in range(TT):
                nc.scalar.activation(psum[:, 2, :], kv["ckv"][:, t, :], ACT.Square,
                                     accum_out=sums[:, 2 + t:3 + t]).then_inc(cq_sq, 1)
                act.wait_ge(cq_sq, 3 + t)
            nc.scalar.activation(rstd[:, 0:2], sums[:, 0:2], ACT.Sqrt, bias=epst[:, 0:1], scale=1.0 / Q_RANK).then_inc(cq_root, 1)
            nc.scalar.activation(rstd[:, 2:6], sums[:, 2:6], ACT.Sqrt, bias=epst[:, 0:1], scale=1.0 / KV_RANK).then_inc(cq_root, 1)
            for n in range(8):
                act.wait_ge(lat_turned, n + 1)
                for i in range(2 if n < 4 else 1):
                    w = par2[:, 64 + 2 * n + i:65 + 2 * n + i] if n < 4 else par2[:, 72 + n - 4:73 + n - 4]
                    width = S if n < 4 else TT * P
                    seg = slice(i * width, (i + 1) * width)
                    dst = hT[:, 0, 0, n, seg] if n < 4 else hT[:, 1, 0, n - 4, :]
                    a = nc.scalar.activation(dst, psum[:, n, seg], ACT.Copy, scale=w)
                a.then_inc(lat_hi, 1)
            for t in range(2):
                nc.scalar.activation(kv["z"][:, t, :], kv["z"][:, t, :], ACT.Silu).then_inc(silu_done, 1)
            nc.scalar.activation(kv["mo"], kv["mo"], ACT.Sigmoid).then_inc(silu_done, 1)
            act.wait_ge(kr_turned, 1)
            nc.scalar.copy(A["krT"], psum[:, 0, :]).then_inc(krT_ready, 1)

            with act.Fori(0, PAIRS) as hp:
                for t in range(3):
                    act.wait_ge(landed[IN][t], hp * 16 + 16 * (IN_RAW // RAW + 1))
                    width = 384 if t < 2 else 512
                    for k in range(KT):
                        n = KT * t + k
                        act.wait_ge(chunk_used, hp * MLA_CHUNKS + (IN_CHUNKS + n + 1 - PART))
                        nc.scalar.copy(part[:, n % PART, 0, 0:width], raw[:, t, k, 0:width]).then_inc(hi_done, 1)
                act.wait_ge(chunk_used, hp * MLA_CHUNKS + (IN_CHUNKS + 8))
                act.wait_ge(s_filled, hp * 4 + 1)
                nc.scalar.copy(A["qnT"], psum[:, 0:2, 0:S]).then_inc(qn_copied, 1)
                act.wait_ge(chunk_used, hp * MLA_CHUNKS + (IN_CHUNKS + 12))
                nc.scalar.copy(A["knT"], psum[:, 4:6, :]).then_inc(kn_copied, 1)
                act.wait_ge(qr_turned, hp + 2)
                nc.scalar.copy(A["qrT"], psum[:, 2, 0:S]).then_inc(qrT_copied, 1)
                for i in range(4):
                    act.wait_ge(negm_ready, hp * 4 + i + 1)
                    act.wait_ge(p_turned, hp * 4 + 1)
                    act.wait_ge(rinv_ready, hp * 4 + 1)
                    nc.scalar.activation(prob[:, i], psum[:, 2 + i, :], ACT.Exp, bias=negm[:, i:i + 1], scale=MLA_SCALE,
                                         accum_out=rows_s[:, i:i + 1]).then_inc(p_ready, 1)

            act.wait_ge(g_step, 1)
            nc.scalar.activation(R["G"][0:MLH], R2["lf"][0:MLH], ACT.Abs).then_inc(gabs, 1)
            act.wait_ge(gabs, 1)
            nc.scalar.activation(R["M"][0:MLH], R["G"][0:MLH], ACT.Exp, scale=-1.0).then_inc(g_exp, 1)
            act.wait_ge(g_exp, 1)
            nc.scalar.activation(R["G"][0:MLH], R["M"][0:MLH], ACT.Ln, bias=epst[0:MLH, 1:2]).then_inc(g_ln, 1)
            act.wait_ge(gt_turned, 1)
            nc.scalar.copy(Gt[:], psum[:, 4, 0:64].rearrange("p (a h) -> p a h", a=8)).then_inc(gt_ready, 1)
            nc.scalar.activation(Et[:], psum[:, 4, 64:96].rearrange("p (a h) -> p a h", a=4), ACT.Exp).then_inc(et_ready, 1)
            def head_in(h, par):
                act.wait_ge(ml_turned, h + 2)
                nc.scalar.activation(L["kT"][0:DQK], psum[0:DQK, 0, :], ACT.Copy, scale=ML_SCALE).then_inc(ml_copied, 1)
                nc.scalar.copy(L["qT"][0:DQK], psum[0:DQK, 1, 0:S]).then_inc(ml_copied, 1)
                if not isinstance(h, int) or h > 1:
                    act.wait_ge(h_filled, h)
                nc.scalar.copy(vst[par][:, :, 0:MLV], kv["mv"][:, :, bass.ds(h * MLV, MLV)]).then_inc(ml_copied, 1)

            def weights(h, par):
                for d in range(2):
                    act.wait_ge(arg_done, h * 2 + d + 1)
                    nc.scalar.activation(wts[par][:, d], wts[par][:, d], ACT.Exp).then_inc(w_exp, 1)

            def squares(h):
                act.wait_ge(h_ready, h + 2)
                act.wait_ge(h_kept, h + 1)
                act.wait_ge(h_sq, h * 2 + 1)
                for t in range(2):
                    nc.scalar.activation(hf[:, t * MLV:(t + 1) * MLV], L["H"][:, t, :], ACT.Square,
                                         accum_out=ssh[:, t:t + 1]).then_inc(h_sq, 1)

            def head_step(h, par):
                head_in(h + 1, 1 - par)
                if not isinstance(h, int) or h > 0:
                    squares(h - 1)
                weights(h + 1, 1 - par)

            act.wait_ge(et_ready, 1)
            head_in(0, 0)
            weights(0, 0)
            heads(act, head_step, 0)
            squares(MLH - 2)
            for i in range(8):
                act.wait_ge(pooled, i + 1)
                nc.scalar.copy(poolT[:, i, :], psum[:, i % 4, 0:S]).then_inc(pooled_copied, 1)
            squares(MLH - 1)
            act.wait_ge(h_kept, MLH + 1)
            nc.scalar.activation(rall[:], ssall[:], ACT.Sqrt, bias=epst[:, 0:1], scale=1.0 / MLV).then_inc(ml_root, 1)

            for k in range(KT):
                turn(OUT, 0, 0, k, IN_TR + k, IN_VECS + 1)
            groups(act, OUT, group)

            act.wait_ge(e_step, 16)
            for t in range(2):
                for n in range(8):
                    act.wait_ge(e_sq, t * 8 + n)
                    nc.scalar.activation(modsb[:], place_of("y", n * W, W, 0, OUT)[:, t, :], ACT.Square,
                                         accum_out=rall[:, n, t:t + 1]).then_inc(e_sq, 1)
            act.wait_ge(e_rstd, 1)
            nc.scalar.activation(rstd[:, 0:2], sums[:, 0:2], ACT.Sqrt, bias=epst[:, 0:1], scale=1.0 / D).then_inc(e_root, 1)

        @block.vector
        def _(dve):
            for s in (o_stored, rinv_ready, q_roped, pT_ready, h_kept, h_ready, w_mul):
                dve.sem_inc(s, 1)
            nc.vector.memset(epst[:, 0:1], EPS).then_inc(eps_set, 1)
            nc.vector.memset(epst[:, 1:2], 1.0).then_inc(eps_set, 1)
            nc.vector.memset(MOD, 0.0).then_inc(mod_zero, 1)
            nc.vector.memset(colsc[:, 0:AT_ML // P], 1.0).then_inc(eps_set, 1)
            dve.wait_ge(tr_filled, 1)
            nc.vector.tensor_copy(par1[:], TR[:, 0:P]).then_inc(par_ready, 1)
            dve.wait_ge(par_ready, 1)
            nc.vector.tensor_scalar(par1[:, 32:64], par1[:, 32:64], 1.0, None, ALU.add).then_inc(tr_read, 1)
            dve.wait_ge(tr_filled, 2)
            nc.vector.tensor_copy(par2[:], TR[:, 0:96]).then_inc(par_ready, 1)
            dve.wait_ge(par_ready, 2)
            dve.wait_ge(tr_read, 1)
            nc.vector.tensor_copy(colsc[:, AT_ML // P:32], par2[:, 76:96]).then_inc(tr_read, 1)
            dve.wait_ge(rms_root, 1)
            nc.vector.memset(place_of("z", D - W, W, 0, IN), 0.0).then_inc(eps_set, 1)
            nc.vector.reciprocal(rstd[:, 0:4], rstd[:, 0:4]).then_inc(rstd_ready, 1)

            def vec(kind, g, use, vecs):
                src = TR[:, 0:8].rearrange("p (k j) -> p k j", j=2)
                dve.wait_ge(tr_filled, use + 1)
                if kind == GATE:
                    nc.vector.tensor_tensor(gateK[:, bass.ds(g * KT, KT)], src[:, :, 0], par1[:, bass.ds(g * KT + 64, KT)],
                                            ALU.add).then_inc(vec_ready, 1)
                else:
                    base = 0 if kind == SHIFT else 32
                    bias = par1[:, bass.ds(g * KT + base, KT)].unsqueeze(2).to_broadcast([P, KT, 2])
                    if not isinstance(g, int) or g > 0:
                        dve.wait_ge(hiT_done, g * KT)
                        dve.wait_ge(full_done, g * KT)
                    if kind == SHIFT:
                        nc.vector.tensor_tensor(shiftv[:], src, bias, ALU.add).then_inc(vec_ready, 1)
                    else:
                        nc.vector.tensor_tensor(scalet[:], src, bias, ALU.add).then_inc(scale_tmp, 1)
                        dve.wait_ge(scale_tmp, g + 1)
                        w = par1[:, bass.ds(g * KT + 96, KT)].unsqueeze(2).to_broadcast([P, KT, 2])
                        nc.vector.tensor_tensor(scalev[:], scalet[:], w, ALU.mult).then_inc(vec_ready, 1)
                dve.wait_ge(vec_ready, vecs + 1)
                dve.sem_inc(tr_read, 1)

            def turn(pr, g, buf, k, use, count):
                dve.wait_ge(tr_filled, use + 1)
                dve.wait_ge(loT_done, count)
                dve.wait_ge(hiT_done, count + 1)
                for i in range(2 if pr is IN else 1):
                    seg = slice(i * S, (i + 1) * S)
                    if pr is IN:
                        a = nc.vector.tensor_scalar(hf[:, seg], TR[:, seg], scalev[:, k, i:i + 1], shiftv[:, k, i:i + 1],
                                                    ALU.mult, ALU.add)
                    else:
                        a = nc.vector.tensor_scalar(hf[:, seg], TR[:, seg], scalev[:, k, 0:1], None, ALU.mult)
                a.then_inc(full_done, 1)
                dve.wait_ge(full_done, count + 1)
                n = 2 * S if pr is IN else S
                nc.vector.tensor_tensor(hT[:, buf, 1, k, 0:n], hf[:, 0:n], hT[:, buf, 0, k, 0:n].bitcast(F32),
                                        ALU.subtract).then_inc(loT_done, 1)
                dve.wait_ge(loT_done, count + 1)
                dve.sem_inc(tr_read, 1)

            def lows(pr, slot, j, g, width):
                for k in range(KT):
                    place = (KT * j + k) % PART
                    dve.wait_ge(hi_done, pr.chunk(j, k, g))
                    nc.vector.tensor_tensor(part[:, place, 1, 0:width], raw[:, slot, k, 0:width],
                                            part[:, place, 0, 0:width].bitcast(F32), ALU.subtract).then_inc(lo_done, 1)

            def add(pr, j, g, first):
                name, col, _, width = pr.tiles[j]
                dve.wait_ge(chunk_used, pr.chunk(j, KT - 1, g))
                q0, n = pr.pair[j]
                for i in range(n):
                    b = banks(q0 + i)
                    dst = place_of(name, col, width, i, pr)
                    if first:
                        nc.vector.tensor_copy(dst, psum[:, b:b + 2, 0:width]).then_inc(added, 1)
                    else:
                        dve.wait_ge(added, g * pr.npairs + (pr.pair0 - pr.npairs + q0 + i + 1))
                        nc.vector.tensor_tensor(dst, dst, psum[:, b:b + 2, 0:width], ALU.add).then_inc(added, 1)

            def mix_mlstm(h):
                for t in range(2):
                    dst = kv["z"][:, t, AT_ML + h * MLV:AT_ML + (h + 1) * MLV]
                    nc.vector.scalar_tensor_tensor(out=dst, in0=kv["mo"][:, t, h * MLV:(h + 1) * MLV],
                                                   scalar=rall[:, h, t:t + 1], in1=dst, op0=ALU.mult,
                                                   op1=ALU.mult).then_inc(ml_mixed, 1)

            def group(pr, g, buf, first, last):
                _, _, others = turn_events(pr, last)
                for idx, item in enumerate(pr.order[last]):
                    if item[0] == "m":
                        continue
                    j = item[1]
                    if pr is OUT and j == 1 and not last:
                        dve.wait_ge(hiT_done, g * KT + OUT.hT0)
                        dve.wait_ge(full_done, g * KT + OUT.hT0)
                        nc.vector.tensor_copy(scalev[:, :, 0], colsc[:, bass.ds(g * KT + KT, KT)]).then_inc(vec_ready, 1)
                        dve.wait_ge(vec_ready, g + IN_VECS + 2)
                    lows(pr, pr.slot(idx), j, g, pr.tiles[j][3])
                    if pr is OUT and first:
                        mix_mlstm(j)
                    if j > 0:
                        add(pr, j - 1, g, first)
                    elif not first:
                        add(pr, pr.n - 1, g - 1, False)
                        for what, number, use in turn_events(pr, False)[2].get(pr.n, ()):
                            vec(number, g - 1, g * pr.ntr + (pr.tr0 - pr.ntr + use), g * 3 + 1)
                    for what, number, use in others.get(j, ()):
                        if what == "turn":
                            turn(pr, g + 1, 1 - buf, number, g * pr.ntr + (pr.tr0 + use), g * KT + (pr.hT0 + number))
                        elif number == GATE:
                            vec(GATE, g, g * pr.ntr + (pr.tr0 + use), g * 3 + 2)
                        else:
                            vec(number, g + 1, g * pr.ntr + (pr.tr0 + use), g * 3 + (2 + number))
                if last:
                    add(pr, pr.n - 1, g, False)

            vec(SHIFT, 0, 2, 0)
            vec(SCALE, 0, 3, 1)
            for k in range(KT):
                turn(IN, 0, 0, k, 4 + k, k)
            dve.wait_ge(eps_set, 4)
            groups(dve, IN, group)

            dve.wait_ge(cq_root, 2)
            nc.vector.reciprocal(rstd[:, 0:6], rstd[:, 0:6]).then_inc(cq_rstd, 1)
            dve.wait_ge(cq_rstd, 1)
            for name, r in (("cq", 0), ("ckv", 2)):
                for t in range(KEPT[name][0]):
                    nc.vector.tensor_scalar(kv[name][:, t, :], kv[name][:, t, :], rstd[:, r + t:r + t + 1], None,
                                            ALU.mult).then_inc(cq_scaled, 1)
            for n in range(8):
                dve.wait_ge(lat_turned, n + 1)
                dve.wait_ge(lat_lo, n)
                dve.wait_ge(lat_hi, n + 1)
                for i in range(2 if n < 4 else 1):
                    w = par2[:, 64 + 2 * n + i:65 + 2 * n + i] if n < 4 else par2[:, 72 + n - 4:73 + n - 4]
                    width = S if n < 4 else TT * P
                    seg = slice(i * width, (i + 1) * width)
                    a = nc.vector.tensor_scalar(hf[:, seg], psum[:, n, seg], w, None, ALU.mult)
                a.then_inc(lat_full, 1)
                dve.wait_ge(lat_full, n + 1)
                b, k = (0, n) if n < 4 else (1, n - 4)
                nc.vector.tensor_tensor(hT[:, b, 1, k, :], hf[:], hT[:, b, 0, k, :].bitcast(F32),
                                        ALU.subtract).then_inc(lat_lo, 1)

            k1, k2 = kv["kg"][:, 0:2, 0:32], kv["kg"][:, 0:2, 32:64]
            tmp = A["qr"].rearrange("p t e c -> p (t e c)").rearrange("p (n t c) -> p n t c", n=4, t=2)
            for n, (a, b) in enumerate(((k1, cosv), (k2, sinv), (k1, sinv), (k2, cosv))):
                nc.vector.tensor_tensor(tmp[:, n], a, b, ALU.mult).then_inc(kr_tmp, 1)
            dve.wait_ge(kr_tmp, 4)
            nc.vector.tensor_tensor(k1, tmp[:, 0], tmp[:, 1], ALU.subtract).then_inc(kr_roped, 1)
            nc.vector.tensor_tensor(k2, tmp[:, 2], tmp[:, 3], ALU.add).then_inc(kr_roped, 1)

            dve.wait_ge(kr_roped, 2)
            dve.wait_ge(lat_lo, 8)
            for e in range(2):
                nc.vector.tensor_copy(key2[:, :, e, :], kv["kg"][:, :, 0:ROPE]).then_inc(kr_roped, 1)

            dve.wait_ge(kr_turned, 1)
            dve.wait_ge(silu_done, 2)
            with dve.Fori(0, PAIRS) as hp:
                for n in range(MLA_CHUNKS):
                    width = 384 if n < 8 else 512
                    dve.wait_ge(hi_done, hp * MLA_CHUNKS + (IN_CHUNKS + n + 1))
                    nc.vector.tensor_tensor(part[:, n % PART, 1, 0:width], raw[:, n // KT, n % KT, 0:width],
                                            part[:, n % PART, 0, 0:width].bitcast(F32), ALU.subtract).then_inc(lo_done, 1)
                dve.wait_ge(chunk_used, hp * MLA_CHUNKS + (IN_CHUNKS + 8))
                dve.wait_ge(qr_turned, hp + 1)
                q = psum[:, 2:4, 0:2 * ROPE].rearrange("p t (e c) -> p t e c", e=2)
                cb = cosv.unsqueeze(2).to_broadcast([P, 2, 2, 32])
                sb_ = sinv.unsqueeze(2).to_broadcast([P, 2, 2, 32])
                r1, r2, ra = A["qr"][:, :, :, 0:32], A["qr"][:, :, :, 32:64], A["ra"]
                nc.vector.tensor_tensor(r1, q[:, :, :, 0:32], cb, ALU.mult).then_inc(q_tmp, 1)
                nc.vector.tensor_tensor(r2, q[:, :, :, 0:32], sb_, ALU.mult).then_inc(q_tmp, 1)
                dve.wait_ge(q_roped, hp * 2 + 1)
                nc.vector.tensor_tensor(ra, q[:, :, :, 32:64], sb_, ALU.mult).then_inc(q_tmp, 1)
                dve.wait_ge(q_tmp, hp * 4 + 3)
                nc.vector.tensor_tensor(r1, r1, ra, ALU.subtract).then_inc(q_roped, 1)
                dve.wait_ge(q_roped, hp * 2 + 2)
                nc.vector.tensor_tensor(ra, q[:, :, :, 32:64], cb, ALU.mult).then_inc(q_tmp, 1)
                dve.wait_ge(q_tmp, hp * 4 + 4)
                nc.vector.tensor_tensor(r2, r2, ra, ALU.add).then_inc(q_roped, 1)
                dve.wait_ge(chunk_used, hp * MLA_CHUNKS + (IN_CHUNKS + 12))
                dve.wait_ge(o_filled, hp * 4 + 1)
                nc.vector.tensor_copy(A["v"][:, 0:2], psum[:, 6:8, 0:2 * DV]).then_inc(v_copied, 1)
                nc.vector.tensor_copy(A["v"][:, 2:4], psum[:, 0:2, 0:2 * DV]).then_inc(v_copied, 1)
                for i in range(4):
                    dve.wait_ge(s_filled, hp * 4 + i + 2)
                    dve.wait_ge(p_ready, hp * 4 + 1)
                    nc.vector.tensor_reduce(negm[:, i:i + 1], psum[:, 2 + i, :], AX_X, ALU.max, negate=True).then_inc(max_done, 1)
                    dve.wait_ge(max_done, hp * 4 + i + 1)
                    nc.vector.tensor_scalar(negm[:, i:i + 1], negm[:, i:i + 1], MLA_SCALE, None, ALU.mult).then_inc(negm_ready, 1)

                def probs_out(i):
                    dve.wait_ge(p_turned, hp * 4 + i + 2)
                    dve.wait_ge(o_filled, hp * 4 + max(i - 1, 0) + 1)
                    nc.vector.tensor_copy(probT[i % 2][:], psum[:, 6 + i % 2, :]).then_inc(pT_ready, 1)

                def head_out(i):
                    dve.wait_ge(p_ready, hp * 4 + i + 2)
                    dve.wait_ge(o_stored, hp * 4 + 1)
                    nc.vector.reciprocal(rinv[:, i:i + 1], rows_s[:, i:i + 1]).then_inc(rinv_ready, 1)
                    dve.wait_ge(rinv_ready, hp * 4 + i + 2)
                    dve.wait_ge(o_filled, hp * 4 + i + 2)
                    dst = kv["z"][:, i % 2, bass.ds(hp * 256 + (i // 2) * 128, DV)]
                    nc.vector.scalar_tensor_tensor(out=dst, in0=psum[:, i % 2, 0:DV], scalar=rinv[:, i:i + 1], in1=dst,
                                                   op0=ALU.mult, op1=ALU.mult).then_inc(o_stored, 1)

                probs_out(0)
                probs_out(1)
                head_out(0)
                probs_out(2)
                head_out(1)
                probs_out(3)
                head_out(2)
                head_out(3)

            li, lf, G, M = R2["li"][0:MLH], R2["lf"][0:MLH], R["G"][0:MLH], R["M"][0:MLH]
            ones = hf[0:MLH, :]
            steps = [0]

            def step(instruction):
                instruction.then_inc(g_step, 1)
                steps[0] += 1

            dve.wait_ge(g_turned, 1)
            dve.wait_ge(p_turned, 4 * PAIRS + 1)
            for d in range(2):
                nc.vector.tensor_scalar(li[:, d, :], psum[0:MLH, d, :], bif[:, d:d + 1], None, ALU.add)
            nc.vector.tensor_scalar(lf[:, 0, :], psum[0:MLH, 2, :], bif[:, 2:3], None, ALU.add)
            step(nc.vector.tensor_scalar(lf[:, 1, :], psum[0:MLH, 3, :], bif[:, 3:4], None, ALU.add))
            step(nc.vector.memset(ones, 1.0))
            dve.wait_ge(g_ln, 1)
            dve.wait_ge(g_step, 2)
            step(nc.vector.scalar_tensor_tensor(out=lf, in0=lf, scalar=0.0, in1=G, op0=ALU.min, op1=ALU.subtract))
            dve.wait_ge(g_step, 3)

            def runs(dst, src0, src1, op0, op1, start):
                step(nc.vector.tensor_tensor_scan(dst[:, 0, :], src0(0, slice(0, 512), False), src1[:, 0, :], start, op0, op1))
                step(nc.vector.tensor_tensor_scan(dst[:, 1, 0:S][:, ::-1], src0(1, slice(0, S), True),
                                                  src1[:, 1, 0:S][:, ::-1], start, op0, op1))
                dve.wait_ge(g_step, steps[0])
                step(nc.vector.tensor_tensor_scan(dst[:, 1, S:2 * S][:, ::-1], src0(1, slice(S, 2 * S), True),
                                                  src1[:, 1, S:2 * S][:, ::-1], dst[:, 1, 0:1], op0, op1))
                dve.wait_ge(g_step, steps[0])

            runs(M, lambda d, seg, back: ones[:, 0:seg.stop - seg.start], lf, ALU.mult, ALU.add, 0.0)
            step(nc.vector.tensor_tensor(G, li, M, ALU.subtract))
            dve.wait_ge(g_step, steps[0])
            runs(lf, lambda d, seg, back: G[:, d, seg][:, ::-1] if back else G[:, d, seg], G, ALU.max, ALU.max, 0.0)
            step(nc.vector.tensor_scalar(L["negM"][0:MLH], lf[:, :, S:2 * S], -1.0, None, ALU.mult))
            dve.wait_ge(g_step, steps[0])
            step(nc.vector.tensor_tensor(li[:, :, S:2 * S], L["negM"][0:MLH], M[:, :, S:2 * S], ALU.subtract))
            assert steps[0] == G_STEPS

            dve.wait_ge(gt_ready, 1)
            dve.wait_ge(et_ready, 1)

            def pick(h):
                dve.wait_ge(ml_turned, h + 1)
                if not isinstance(h, int) or h > 0:
                    dve.wait_ge(arg_done, h * 2)
                nc.vector.tensor_copy(selh[:], ident[0:MLH, bass.ds(h, 1)].to_broadcast([MLH, P])).then_inc(picked, 1)
                nc.vector.tensor_copy(Gh[:].unsqueeze(2), Gt[:, :, bass.ds(h, 1)]).then_inc(picked, 1)

            def exponents(h, par):
                dve.wait_ge(picked, h * 2 + 2)
                dve.wait_ge(ml_turned, h + 2)
                if not isinstance(h, int) or h > 1:
                    dve.wait_ge(h_filled, h)
                for d in range(2):
                    for s in range(4):
                        a = nc.vector.tensor_scalar(wts[par][:, d, s, :], psum[:, 2, d * S:(d + 1) * S],
                                                    Gh[:, d * 4 + s:d * 4 + s + 1], 0.0, ALU.add, ALU.min)
                    a.then_inc(arg_done, 1)

            def times_scores(h, par):
                sT = psum[:, 3:5, :].rearrange("p b (s t) -> p (b s) t", s=2)
                dve.wait_ge(sT_filled, h + 1)
                for d in range(2):
                    dve.wait_ge(w_exp, h * 2 + d + 1)
                    nc.vector.tensor_tensor(wts[par][:, d], wts[par][:, d], sT, ALU.mult).then_inc(w_mul, 1)

            def keep_squares(h):
                dve.wait_ge(h_sq, h * 2 + 3)
                nc.vector.tensor_copy(ssall[:, bass.ds(h, 1), :], ssh[:].unsqueeze(1)).then_inc(h_kept, 1)

            def head_out(h, par):
                nc.vector.tensor_copy(Eh[:].unsqueeze(2), Et[:, :, bass.ds(h, 1)]).then_inc(e_picked, 1)
                dve.wait_ge(h_filled, h + 2)
                sums_of = [psum[:, b, :].rearrange("p (t c) -> p t c", t=2) for b in ((5, 7)[par], 6)]
                nc.vector.tensor_copy(den[:, 0:2].unsqueeze(2), sums_of[0][:, :, MLV:MLV + 1])
                nc.vector.tensor_copy(den[:, 2:4].unsqueeze(2), sums_of[1][:, :, MLV:MLV + 1]).then_inc(h_step, 1)
                if not isinstance(h, int) or h > 0:
                    keep_squares(h - 1)
                dve.wait_ge(h_step, h * 7 + 1)
                nc.vector.tensor_scalar(dent[:], den[:], -1.0, None, ALU.mult).then_inc(h_step, 1)
                dve.wait_ge(h_step, h * 7 + 2)
                nc.vector.tensor_tensor(den[:], den[:], dent[:], ALU.max).then_inc(h_step, 1)
                dve.wait_ge(h_step, h * 7 + 3)
                dve.wait_ge(e_picked, h + 1)
                nc.vector.tensor_tensor(den[:], den[:], Eh[:], ALU.max).then_inc(h_step, 1)
                dve.wait_ge(h_step, h * 7 + 4)
                nc.vector.reciprocal(dent[:], den[:]).then_inc(h_step, 1)
                dve.wait_ge(h_step, h * 7 + 5)
                dve.wait_ge(h_sq, h * 2 + 1)
                H = L["H"]
                for t in range(2):
                    a = nc.vector.tensor_scalar(H[:, t, :], sums_of[0][:, t, 0:MLV], dent[:, t:t + 1], None, ALU.mult)
                a.then_inc(h_step, 1)
                dve.wait_ge(h_step, h * 7 + 6)
                for t in range(2):
                    a = nc.vector.scalar_tensor_tensor(out=H[:, t, :], in0=sums_of[1][:, t, 0:MLV],
                                                       scalar=dent[:, 2 + t:3 + t], in1=H[:, t, :], op0=ALU.mult,
                                                       op1=ALU.add)
                a.then_inc(h_ready, 1)
                dve.wait_ge(h_ready, h + 2)
                mo = kv["mo"][:, :, bass.ds(h * MLV, MLV)]
                nc.vector.tensor_tensor(mo, mo, H, ALU.mult).then_inc(h_step, 1)

            def head_step(h, par):
                exponents(h + 1, 1 - par)
                if not isinstance(h, int) or h < MLH - 2:
                    pick(h + 2)
                times_scores(h + 1, 1 - par)
                head_out(h, par)

            pick(0)
            exponents(0, 0)
            pick(1)
            times_scores(0, 0)
            heads(dve, head_step, 2)
            head_out(MLH - 1, 1)
            for i in range(8):
                dve.wait_ge(pool_filled, i + 1)
                g, t = i // 2, i % 2
                dst = kv["z"][:, t, AT_POOL + g * PC:AT_POOL + (g + 1) * PC]
                nc.vector.tensor_tensor(dst, psum[:, 4 + i % 4, 0:PC], dst, ALU.mult).then_inc(pool_mixed, 1)
            keep_squares(MLH - 1)
            dve.wait_ge(ml_root, 1)
            nc.vector.reciprocal(rall[:], rall[:]).then_inc(ml_rstd, 1)
            dve.wait_ge(ml_rstd, 1)
            dve.wait_ge(h_step, 7 * MLH)

            nc.vector.memset(place_of("y", D - W, W, 0, OUT), 0.0).then_inc(eps_set, 1)
            nc.vector.tensor_copy(scalev[:, :, 0], colsc[:, 0:KT]).then_inc(vec_ready, 1)
            dve.wait_ge(vec_ready, IN_VECS + 1)
            dve.wait_ge(eps_set, 5)
            for k in range(KT):
                turn(OUT, 0, 0, k, IN_TR + k, KT * NG + k)
            groups(dve, OUT, group)

            dve.wait_ge(gate_turned, 1)
            nc.vector.tensor_copy(gateR[:], psum[0:32, TR_BANK, 0:P]).then_inc(gate_row, 1)
            dve.wait_ge(gate_filled, 1)
            dve.wait_ge(xe_in, 32)
            dve.wait_ge(added, IN_PAIRS + OUT.npairs * NG)
            for n in range(8):
                y = place_of("y", n * W, W, 0, OUT)
                gate = psum[:, n, :].unsqueeze(1).to_broadcast([P, 2, W])
                nc.vector.tensor_tensor(y, y, gate, ALU.mult).then_inc(e_step, 1)
            for n in range(8):
                dve.wait_ge(e_step, n + 1)
                y = place_of("y", n * W, W, 0, OUT)
                nc.vector.tensor_tensor(y, y, kv["z"][:, :, n * W:(n + 1) * W], ALU.add).then_inc(e_step, 1)
            dve.wait_ge(e_sq, 16)
            nc.vector.tensor_reduce(sums[:, 0:2], rall[:].rearrange("p n t -> p t n"), AX_X, ALU.add).then_inc(e_rstd, 1)
            dve.wait_ge(e_root, 1)
            nc.vector.reciprocal(rstd[:, 0:2], rstd[:, 0:2]).then_inc(e_rstd, 1)
            dve.wait_ge(e_rstd, 2)
            dve.wait_ge(fw_in, 16)
            for t in range(2):
                for n in range(8):
                    y = place_of("y", n * W, W, 0, OUT)[:, t, :]
                    nc.vector.scalar_tensor_tensor(out=y, in0=y, scalar=rstd[:, t:t + 1], in1=free16[:, n * W:(n + 1) * W],
                                                   op0=ALU.mult, op1=ALU.mult).then_inc(e_out, 1)

        @block.tensor
        def _(pe):
            def three(dst, left, right, first, last):
                passes = ((0, 0), (0, 1), (1, 0))
                for n, (a, b) in enumerate(passes):
                    m = nc.tensor.matmul(dst, left(a), right(b), start=first and n == 0, stop=last and n == 2)
                return m

            def mod_tile(kc, slot, landed_at, copied):
                pe.wait_ge(landed[IN][slot], landed_at)
                if kc == 0:
                    pe.wait_ge(mod_copied, copied)
                for q in range(KT):
                    m = nc.tensor.matmul(psum[32 * q:32 * q + 2, MOD_BANK, :], cT[:, :, KT * kc + q], raw[:, slot, q, :],
                                         start=kc == 0, stop=kc == 7)
                m.then_inc(mod_used, 1)

            def vec(use, copied):
                pe.wait_ge(mod_copied, copied)
                pe.wait_ge(tr_read, use)
                for k in range(KT):
                    m = nc.tensor.matmul(TR[:, 2 * k:2 * k + 2], modsb[:, k * P:(k + 1) * P], sel2, start=True, stop=True)
                m.then_inc(tr_filled, 1)

            def turn(pr, k, use, ready):
                pe.wait_ge(xs_ready, ready)
                pe.wait_ge(tr_read, use)
                for t in range(TT if pr is IN else 2):
                    m = nc.tensor.transpose(TR[:, t * P:(t + 1) * P], xs[:, t, k * P:(k + 1) * P], ident)
                m.then_inc(tr_filled, 1)

            def column_tile(pr, j, g, buf, first):
                name, _, _, width = pr.tiles[j]
                q0, n = pr.pair[j]
                for i in range(n):
                    if (need := pr.pair_free(q0 + i, g, first)) is not None:
                        pe.wait_ge(added, need)
                for k in range(KT):
                    place = (KT * j + k) % PART
                    pe.wait_ge(lo_done, pr.chunk(j, k, g))
                    for i in range(n):
                        for t in range(2):
                            tok = slice((2 * i + t) * P, (2 * i + t + 1) * P)
                            m = three(psum[:, banks(q0 + i) + t, 0:width], lambda a: hT[:, buf, a, k, tok],
                                      lambda b: part[:, place, b, 0:width], k == 0, k == KT - 1)
                    m.then_inc(chunk_used, 1)

            def group(pr, g, buf, first, last):
                events, _, _ = turn_events(pr, last)
                pe.wait_ge(loT_done, g * KT + pr.hT0)
                for idx, item in enumerate(pr.order[last]):
                    if item[0] == "m":
                        kind = 0 if last else item[1]
                        mod_tile(item[2], pr.slot(idx), pr.landed_at(idx, g), g * 3 + (2 + kind))
                        continue
                    j = item[1]
                    column_tile(pr, j, g, buf, first)
                    for what, number, use in events.get(j, ()):
                        use = g * pr.ntr + (pr.tr0 + use)
                        if what == "vec":
                            kind = 0 if last else number
                            vec(use, g * 3 + (3 + kind))
                        else:
                            turn(pr, number, use, g * TT + 2 * TT if pr is IN else g + (TT * NG + 2))

            for s in (s_filled, p_turned, qr_turned, o_filled, ml_turned, h_filled):
                pe.sem_inc(s, 1)
            pe.wait_ge(par_in, 16 * PARAM_LOADS)
            for n, rows in enumerate((P, 96)):
                pe.wait_ge(tr_read, n)
                nc.tensor.transpose(TR[:, 0:rows], par_rows[0:rows, n, :], ident[0:rows, 0:rows]).then_inc(tr_filled, 1)
            pe.wait_ge(c_ready, 1)
            pe.wait_ge(mod_zero, 1)
            for n in range(PRO_MODS):
                mod_tile(n % 8, n % RAW, 16 * (n // RAW + 1), n // 8)
                if n == 8:
                    vec(2, 1)
            vec(3, 2)
            for k in range(KT):
                turn(IN, k, 4 + k, TT)
            groups(pe, IN, group)

            pe.wait_ge(added, IN_PAIRS)
            pe.wait_ge(mod_copied, IN_VECS)
            pe.wait_ge(tr_read, IN_TR)
            for n in range(8):
                pe.wait_ge(cq_scaled, 2 if n < 4 else 6)
                for i in range(4):
                    if n < 4:
                        src = kv["cq"][:, i % 2, (2 * n + i // 2) * P:(2 * n + i // 2 + 1) * P]
                    else:
                        src = kv["ckv"][:, i, (n - 4) * P:(n - 3) * P]
                    m = nc.tensor.transpose(psum[:, n, i * P:(i + 1) * P], src, ident)
                m.then_inc(lat_turned, 1)
            pe.wait_ge(kr_roped, 4)
            for t in range(TT):
                m = nc.tensor.transpose(psum[:, 0, t * P:(t + 1) * P], key2[:, t].rearrange("p e c -> p (e c)"), ident)
            m.then_inc(kr_turned, 1)
            pe.wait_ge(krT_ready, 1)

            def cqT(a, kk, tok):
                at = (kk % 2) * S
                return hT[:, 0, a, kk // 2, at + tok.start:at + tok.stop]

            with pe.Fori(0, PAIRS) as hp:
                pe.wait_ge(o_stored, hp * 4 + 1)
                pe.wait_ge(p_ready, hp * 4 + 1)
                for n in range(8):
                    pe.wait_ge(lo_done, hp * MLA_CHUNKS + (IN_CHUNKS + n + 1))
                    w = part[:, n % PART]
                    for e in range(2):
                        three(psum[:, e, 0:S], lambda b: w[:, b, e * 192:e * 192 + NOPE], lambda a: cqT(a, n, slice(0, S)),
                              n == 0, n == 7)
                    for t in range(2):
                        m = three(psum[:, 2 + t, 0:2 * ROPE].rearrange("p (e c) -> p e c", e=2),
                                  lambda a: cqT(a, n, slice(t * P, (t + 1) * P)),
                                  lambda b: w[:, b, 0:384].rearrange("p (e c) -> p e c", e=2)[:, :, NOPE:192],
                                  n == 0, n == 7)
                    m.then_inc(chunk_used, 1)
                pe.wait_ge(qn_copied, hp + 1)
                pe.wait_ge(pT_ready, hp * 4 + 1)
                for n in range(KT):
                    pe.wait_ge(lo_done, hp * MLA_CHUNKS + (IN_CHUNKS + 8 + n + 1))
                    w = part[:, n % PART]
                    for e in range(2):
                        three(psum[:, 4 + e, :], lambda b: w[:, b, e * 256:e * 256 + NOPE], lambda a: hT[:, 1, a, n, :],
                              n == 0, n == KT - 1)
                    for t in range(TT):
                        m = three(psum[:, (6, 7, 0, 1)[t], 0:2 * DV].rearrange("p (e c) -> p e c", e=2),
                                  lambda a: hT[:, 1, a, n, t * P:(t + 1) * P],
                                  lambda b: w[:, b, :].rearrange("p (e c) -> p e c", e=2)[:, :, NOPE:256],
                                  n == 0, n == KT - 1)
                    m.then_inc(chunk_used, 1)
                pe.wait_ge(q_roped, hp * 2 + 3)
                for t in range(2):
                    m = nc.tensor.transpose(psum[:, 2, t * P:(t + 1) * P], A["qr"][:, t].rearrange("p e c -> p (e c)"), ident)
                m.then_inc(qr_turned, 1)
                pe.wait_ge(qrT_copied, hp + 1)
                pe.wait_ge(kn_copied, hp + 1)
                for i in range(4):
                    e, t = i // 2, i % 2
                    q = slice(t * P, (t + 1) * P)
                    nc.tensor.matmul(psum[:, 2 + i, :], A["qnT"][:, e, q], A["knT"][:, e, :], start=True, stop=False)
                    half = slice(e * ROPE, (e + 1) * ROPE)
                    nc.tensor.matmul(psum[:, 2 + i, :], A["qrT"][half, q], A["krT"][half, :], start=False,
                                     stop=True).then_inc(s_filled, 1)

                def turn_probs(i):
                    pe.wait_ge(p_ready, hp * 4 + i + 2)
                    if i < 2:
                        pe.wait_ge(v_copied, hp * 2 + 1)
                    else:
                        pe.wait_ge(pT_ready, hp * 4 + i - 1 + 1)
                    for t in range(TT):
                        m = nc.tensor.transpose(psum[:, 6 + i % 2, t * P:(t + 1) * P], prob[:, i, t * P:(t + 1) * P], ident)
                    m.then_inc(p_turned, 1)

                def head_out(i):
                    pe.wait_ge(pT_ready, hp * 4 + i + 2)
                    if i < 2:
                        pe.wait_ge(v_copied, hp * 2 + 2)
                    else:
                        pe.wait_ge(o_stored, hp * 4 + i - 1 + 1)
                    for t in range(TT):
                        m = nc.tensor.matmul(psum[:, i % 2, 0:DV], probT[i % 2][:, t * P:(t + 1) * P],
                                             A["v"][:, t, (i // 2) * DV:(i // 2 + 1) * DV], start=t == 0, stop=t == TT - 1)
                    m.then_inc(o_filled, 1)

                turn_probs(0)
                turn_probs(1)
                head_out(0)
                turn_probs(2)
                head_out(1)
                turn_probs(3)
                head_out(2)
                head_out(3)

            pe.wait_ge(o_stored, 4 * PAIRS + 1)
            for n in range(4):
                for t in range(TT):
                    at = ((t + 2) % TT) * P
                    m = nc.tensor.transpose(psum[0:MLH, n, at:at + P], kv["kg"][:, t, 64 + n * MLH:64 + (n + 1) * MLH], ident)
            m.then_inc(g_turned, 1)
            pe.wait_ge(g_step, G_STEPS)
            id8 = ident[0:MLH, 0:MLH]
            for n in range(8):
                nc.tensor.transpose(psum[:, 4, n * MLH:(n + 1) * MLH], R["G"][0:MLH, n // 4, (n % 4) * P:(n % 4 + 1) * P], id8)
            for n in range(4):
                m = nc.tensor.transpose(psum[:, 4, 64 + n * MLH:64 + (n + 1) * MLH],
                                        R2["li"][0:MLH, n // 2, S + (n % 2) * P:S + (n % 2 + 1) * P], id8)
            m.then_inc(gt_turned, 1)
            pe.wait_ge(et_ready, 1)
            pe.wait_ge(gt_ready, 1)

            def turn_head(h):
                pe.wait_ge(staged, h * 2 + 4)
                pe.wait_ge(picked, h * 2 + 2)
                if not isinstance(h, int) or h > 0:
                    pe.wait_ge(ml_copied, h * 3 - 1)
                    pe.wait_ge(arg_done, h * 2)
                for s in range(4):
                    nc.tensor.transpose(psum[0:DQK, 0, s * P:(s + 1) * P], L["kst"][:, (s + 2) % 4, :], ident)
                for t in range(2):
                    nc.tensor.transpose(psum[0:DQK, 1, t * P:(t + 1) * P], L["qst"][:, t, :], ident)
                nc.tensor.matmul(psum[:, 2, :], selh[:], L["negM"][0:MLH].rearrange("p d t -> p (d t)"), start=True,
                                 stop=True).then_inc(ml_turned, 1)

            def scores(h):
                pe.wait_ge(ml_copied, h * 3 + 2)
                pe.wait_ge(w_mul, h * 2 + 1)
                for s in range(4):
                    m = nc.tensor.matmul(psum[:, 3 + s // 2, (s % 2) * S:(s % 2 + 1) * S], L["kT"][0:DQK, s * P:(s + 1) * P],
                                         L["qT"][0:DQK, :], start=True, stop=True)
                m.then_inc(sT_filled, 1)

            def values(h, par, d):
                pe.wait_ge(w_ready, h * 2 + d + 1)
                if d == 0:
                    pe.wait_ge(ml_copied, h * 3 + 3)
                    if not isinstance(h, int) or h > 1:
                        pe.wait_ge(h_ready, h)
                else:
                    pe.wait_ge(h_ready, h + 1)
                for t in range(2):
                    seen = [0, 1] + [2 + s for s in range(2) if (s <= t if d == 0 else s >= t)]
                    for s in seen:
                        m = nc.tensor.matmul(psum[:, (5, 7)[par] if d == 0 else 6, t * S:t * S + MLV + 1],
                                             wts[par][:, d, s, t * P:(t + 1) * P], vst[par][:, (s + 2) % 4, 0:MLV + 1],
                                             start=s == seen[0], stop=s == seen[-1])
                if d == 1:
                    m.then_inc(h_filled, 1)

            def head_step(h, par):
                turn_head(h + 1)
                values(h, par, 0)
                scores(h + 1)
                values(h, par, 1)

            turn_head(0)
            scores(0)
            heads(pe, head_step, 0)
            values(MLH - 1, 1, 0)
            values(MLH - 1, 1, 1)

            for slot in range(2):
                pe.wait_ge(landed[OUT][slot], 16)
            pe.wait_ge(w_mul, 2 * MLH + 1)
            for i in range(8):
                g = i // 2
                if i >= 4:
                    pe.wait_ge(pooled_copied, i - 3)
                for s in range(2):
                    m = nc.tensor.matmul(psum[:, i % 4, 0:S], kv["pu"][:, s, i * P:(i + 1) * P], band[:, s, g, :],
                                         start=s == 0, stop=s == 1)
                m.then_inc(pooled, 1)
            for i in range(8):
                g, t = i // 2, i % 2
                pe.wait_ge(pooled_copied, 2 * g + 2)
                if i == 0:
                    pe.wait_ge(h_ready, MLH + 1)
                if i >= 4:
                    pe.wait_ge(pool_mixed, i - 3)
                for cc in range(2):
                    m = nc.tensor.matmul(psum[:, 4 + i % 4, 0:PC], poolT[:, 2 * g + cc, t * P:(t + 1) * P], poolw[:, g, cc, :],
                                         start=cc == 0, stop=cc == 1)
                m.then_inc(pool_filled, 1)

            pe.wait_ge(pooled_copied, 8)
            pe.wait_ge(pool_mixed, 8)
            for k in range(KT):
                turn(OUT, k, IN_TR + k, TT * NG + 1)
            groups(pe, OUT, group)

            pe.wait_ge(added, IN_PAIRS + OUT.npairs * NG)
            pe.wait_ge(tr_read, IN_TR + OUT.ntr * NG)
            nc.tensor.transpose(psum[0:32, TR_BANK, 0:P], gateK[:], ident).then_inc(gate_turned, 1)
            pe.wait_ge(gate_row, 1)
            for k in range(32):
                m = nc.tensor.matmul(psum[:, k // 4, (k % 4) * P:(k % 4 + 1) * P], ident[0:32, k:k + 1].to_broadcast([32, P]),
                                     gateR[:], start=True, stop=True)
            m.then_inc(gate_filled, 1)


def shape_constants():
    f = np.float32
    rows, cols = np.repeat(np.arange(S // GRID_W), GRID_W), np.tile(np.arange(GRID_W), S // GRID_W)
    n = ROPE // 4
    inv = np.power(f(ROPE_BASE), -np.arange(n, dtype=f) / f(n)).astype(f)
    ang = np.concatenate([rows.astype(f)[:, None] * inv, cols.astype(f)[:, None] * inv], axis=1)
    halves = lambda a: np.concatenate([a[0:P], a[P:2 * P]], axis=1)
    pick = (np.arange(P)[:, None] % 32 == np.arange(2)[None, :]).astype(f)
    tables = np.concatenate([np.eye(P, dtype=f), halves(np.cos(ang)), halves(np.sin(ang)), pick], axis=1).astype(f)
    key, query = np.arange(P)[:, None], np.arange(P)[None, :]
    masks = np.concatenate([(key <= query).astype(f), (key >= query).astype(f)], axis=1)
    b = []
    key, query = np.arange(S)[:, None], np.arange(S)[None, :]
    for w in WINDOWS:
        lo, hi = np.clip(query - w // 2, 0, S), np.clip(query + w - w // 2, 0, S)
        mean = ((key >= lo) & (key < hi)).astype(np.float64) / (hi - lo)
        b.append((mean - (key == query)).astype(f))
    b = np.stack(b, axis=1)
    bands = np.stack([b[0:P], b[P:2 * P]], axis=1).reshape(P, -1)
    return {"tables": np.ascontiguousarray(tables), "masks": np.ascontiguousarray(masks),
            "bands": np.ascontiguousarray(bands)}


INS = ["x", "c", "ctx", "c_ctx", "norm_w", "w_mod", "b_mod", "w_in", "q_norm_w", "kv_norm_w", "w_uq", "w_ukv", "ml_b_i",
       "ml_b_f", "ml_norm_w", "pool_w", "pool_scale", "w_out", "final_norm_w"]


def kernel(**inputs):
    import concourse.bacc as bacc
    from concourse.bass_utils import run_bass_kernel_spmd

    nc = bacc.Bacc("TRN2", target_bir_lowering=False, num_devices=1)
    given = {name: np.ascontiguousarray(inputs[name]) for name in INS}
    given.update(shape_constants())
    arrays, args = {}, []
    for name, a in given.items():
        arrays[f"in_{name}"] = a
        args.append(nc.dram_tensor(f"in_{name}", a.shape, mybir.dt.from_np(a.dtype), kind="ExternalInput").ap())
    out = nc.dram_tensor("out_y", (1, S, D), F32, kind="ExternalOutput").ap()
    hybrid_kernel(nc, *args, out)
    r = run_bass_kernel_spmd(nc, [arrays], core_ids=[0])
    return r.results[0]["out_y"]
```

```python
from contextlib import ExitStack

import numpy as np
import concourse.bass as bass
from concourse import mybir

F32 = mybir.dt.float32
F32R = mybir.dt.float32r
ALU = mybir.AluOpType
ACT = mybir.ActivationFunctionType
AX_X = mybir.AxisListType.X

P = 128
D = 4096
S = 256
TT = 4
EPS = 1e-6
GRID_W = 64
ROPE_BASE = 10000.0

HEADS, NOPE, ROPE, DV = 12, 128, 64, 128
PAIRS = HEADS // 2
Q_RANK, KV_RANK = 1024, 512
MLA_SCALE = (NOPE + ROPE) ** -0.5
MLH, DQK, MLV = 8, 96, 192
ML_SCALE = DQK ** -0.5
WINDOWS, PC = (2, 4, 8, 16), 256
AT_ML, AT_POOL = HEADS * DV, HEADS * DV + MLH * MLV

W = 512
KT = 4
NG = D // (KT * P)
RAW = 4
PART = 4
PAIR_BANKS = 3
MOD_BANK, TR_BANK = 6, 7

C_CQ, C_CKV, C_KR, C_MQ, C_MK, C_MV, C_MO, C_GATES, C_PU, C_Z = (
    0, 1024, 1536, 1600, 2368, 3136, 4672, 6208, 6240, 7264)

KEPT = {"z": (2, 4096), "mv": (4, 1536), "mk": (4, 768), "mo": (2, 1536), "mq": (2, 768), "pu": (2, 1024),
        "cq": (2, 1024), "ckv": (4, 512), "kg": (4, 96)}


def places():
    at, out = 0, {}
    for name, (t, w) in KEPT.items():
        out[name] = at
        at += t * w
    return out, at


KEPT_AT, KEPT_SIZE = places()


def in_tiles():
    both = [("ckv", 0, C_CKV, W)]
    both += [("mk", c, C_MK + c, 384) for c in (0, 384)]
    both += [("mv", c, C_MV + c, W) for c in (0, 512, 1024)]
    both += [("kg", 0, C_KR, 96)]
    latent = [("cq", c, C_CQ + c, W) for c in (0, 512)] + [("mq", c, C_MQ + c, 384) for c in (0, 384)]
    latent += [("mo", c, C_MO + c, W) for c in (0, 512, 1024)] + [("pu", c, C_PU + c, W) for c in (0, 512)]
    latent += [("z", c, C_Z + c, W) for c in range(0, D, W)]
    tiles = []
    for i, tile in enumerate(both):
        tiles.append(tile)
        n = len(latent) * (i + 1) // len(both) - len(latent) * i // len(both)
        done = len(tiles) - i - 1
        tiles += latent[done:done + n]
    return tiles


SHIFT, SCALE, GATE = range(3)


class Product:

    def __init__(self, tiles, mods, last_mods, ring, raw0, chunk0, pair0, tr0, hT0, mod0, turn_at):
        self.tiles, self.n, self.ring = tiles, len(tiles), ring
        self.order = (self.place(mods), self.place(last_mods))
        self.pair = []
        at = 0
        for name, *_ in tiles:
            k = KEPT[name][0] // 2 if name in KEPT else 1
            self.pair.append((at, k))
            at += k
        self.npairs, self.nraw, self.nmods = at, len(self.order[0]), len(mods)
        self.ntr = 4 + len(mods) // 8
        self.raw0, self.chunk0, self.pair0, self.tr0, self.hT0, self.mod0 = raw0, chunk0, pair0, tr0, hT0, mod0
        self.turn_at = turn_at

    def place(self, mods):
        out, left = [], list(mods)
        for j in range(self.n):
            if j == self.n - 1:
                out += left
                left = []
            out.append(("w", j))
            if left:
                out.append(left.pop(0))
        return out

    def slot(self, idx):
        return (self.raw0 + idx) % self.ring

    def landed_at(self, idx, g):
        return g * (16 * (self.nraw // self.ring)) + 16 * ((self.raw0 + idx) // self.ring + 1)

    def chunk(self, j, k, g):
        return g * (KT * self.n) + (self.chunk0 + KT * j + k + 1)

    def pair_free(self, q, g, first):
        last = q - PAIR_BANKS
        if q < PAIR_BANKS:
            if first:
                return None
            last = max(i for i in range(self.npairs) if i % PAIR_BANKS == q % PAIR_BANKS) - self.npairs
        return g * self.npairs + (self.pair0 + last + 1)

    def free(self, idx, g, first):
        back = idx - self.ring
        order = self.order[0]
        if back < 0:
            if first:
                return None
            back, g = back + self.nraw, g - 1
        elif isinstance(g, int) and g == NG - 1:
            order = self.order[1]
        kind = order[back]
        if kind[0] == "w":
            return True, self.chunk(kind[1], KT - 1, g)
        return False, g * self.nmods + (self.mod0 + sum(1 for o in order[:back + 1] if o[0] == "m"))


MODS = [("m", kind, kc) for kind in (SHIFT, SCALE, GATE) for kc in range(8)]
PRO_MODS = 16
PRO_TR = 2 + 2 + 4
IN = Product(in_tiles(), MODS, MODS[16:], ring=RAW, raw0=PRO_MODS, chunk0=0, pair0=0, tr0=PRO_TR, hT0=4,
             mod0=PRO_MODS, turn_at=18)
IN_RAW = PRO_MODS + IN.nraw * (NG - 1) + len(IN.order[1])
IN_CHUNKS = KT * IN.n * NG
IN_PAIRS = IN.npairs * NG
IN_TR = PRO_TR + IN.ntr * (NG - 1) + 1
LAST_Z = 3
GATED = sum(1 for t in IN.tiles if t[0] in ("z", "mo"))


def summed(j):
    return IN.npairs * (NG - 1) + sum(IN.pair[j])


RANKS_SUMMED = max(summed(j) for j, t in enumerate(IN.tiles) if t[0] in ("cq", "ckv"))
KG_SUMMED = max(summed(j) for j, t in enumerate(IN.tiles) if t[0] == "kg")
assert RANKS_SUMMED <= summed(4) and KG_SUMMED <= summed(IN.n - 2)
IN_VECS = 2 + 3 * (NG - 1) + 1
MLA_CHUNKS = 12
OUT = Product([("y", n * W, n * W, W) for n in range(D // W)], [], [], ring=RAW, raw0=2,
              chunk0=IN_CHUNKS + MLA_CHUNKS * PAIRS, pair0=IN_PAIRS, tr0=IN_TR + 4, hT0=4 * NG + 4, mod0=0, turn_at=2)
assert IN_RAW % RAW == 0 and IN.nraw % RAW == 0 and OUT.nraw % OUT.ring == 0 and IN.n * KT % PART == 0
PARAM_LOADS = 3 + 6 + 4
Y_POOL = OUT.n - 1
Y_ACT = 4
G_STEPS = 12



def turn_events(pr, last):
    pe, copies, others = {}, {}, {}
    use = 0

    def at(j, what, number):
        nonlocal use
        pe.setdefault(j, []).append((what, number, use))
        others.setdefault(j + 1, []).append((what, number, use))
        use += 1

    if pr.nmods and not last:
        copies[8] = copies[16] = copies[pr.n - 1] = True
        at(8, "vec", SHIFT)
        at(16, "vec", SCALE)
    if pr.nmods and last:
        copies[8] = True
        at(8, "vec", GATE)
    if not last:
        for k in range(KT):
            at(pr.turn_at + k, "turn", k)
        if pr.nmods:
            at(pr.n - 1, "vec", GATE)
    return pe, copies, others


def hybrid_kernel(nc, x, c, ctx, c_ctx, norm_w, w_mod, b_mod, w_in, q_norm_w, kv_norm_w, w_uq, w_ukv, ml_b_i,
                  ml_b_f, ml_norm_w, pool_w, pool_scale, w_out, final_norm_w, tables, masks, bands, out):
    with ExitStack() as stack:
        def sb(name, shape, dt=F32):
            return stack.enter_context(nc.sbuf_tensor(name, shape, dt))

        def sem(name):
            return stack.enter_context(nc.semaphore(name))

        kept = sb("kept", [P, KEPT_SIZE])
        raw = sb("raw", [P, RAW, KT, W])
        part = sb("part", [P, PART, 2, W], F32R)
        hT = sb("hT", [P, 2, 2, KT, TT * P], F32R)
        xs = sb("xs", [P, TT, KT * P])
        modsb = sb("modsb", [P, W])
        hf = sb("hf", [P, W])
        tab = sb("tab", [P, 258])
        cT = sb("cT", [P, 2, 32])
        par1 = sb("par1", [P, P])
        par2 = sb("par2", [P, 96])
        colsc = sb("colsc", [P, 32])
        shiftv = sb("shiftv", [P, KT, 2])
        scalet = sb("scalet", [P, KT, 2])
        scalev = sb("scalev", [P, KT, 2])
        gateK = sb("gateK", [P, 32])
        sums = sb("sums", [P, 8])
        rstd = sb("rstd", [P, 8])
        epst = sb("epst", [P, 2])
        bif = sb("bif", [MLH, 4])
        negm = sb("negm", [P, 4])
        rows_s = sb("rows_s", [P, 4])
        rinv = sb("rinv", [P, 4])
        Gt = sb("Gt", [P, 8, MLH])
        Et = sb("Et", [P, 4, MLH])
        Gh = sb("Gh", [P, 8])
        Eh = sb("Eh", [P, 4])
        den = sb("den", [P, 4])
        dent = sb("dent", [P, 4])
        selh = sb("selh", [MLH, P])
        ssh = sb("ssh", [P, 2])
        ssall = sb("ssall", [P, MLH, 2])
        rall = sb("rall", [P, MLH, 2])

        ident = tab[:, 0:128]
        cosv = tab[:, 128:192].rearrange("p (t f) -> p t f", t=2)
        sinv = tab[:, 192:256].rearrange("p (t f) -> p t f", t=2)
        sel2 = tab[:, 256:258]
        par_rows = hf[:, 0:256].rearrange("p (a c) -> p a c", a=2)

        def keep(name):
            t, w = KEPT[name]
            return kept[:, KEPT_AT[name]:KEPT_AT[name] + t * w].rearrange("p (t c) -> p t c", t=t)

        kv = {name: keep(name) for name in KEPT}
        xfull = kept[:, 0:4 * D].rearrange("p (t c) -> p t c", t=4)

        def arena(base, spec):
            views, at = {}, 0
            for name, shape in spec.items():
                size = int(np.prod(shape))
                v = base[:, at:at + size]
                if len(shape) == 2:
                    v = v.rearrange("p (a b) -> p a b", a=shape[0])
                elif len(shape) == 3:
                    v = v.rearrange("p (a b c) -> p a b c", a=shape[0], b=shape[1])
                views[name] = v
                at += size
            return views

        free16 = kept[:, KEPT_AT["cq"]:KEPT_AT["cq"] + 4096]
        free8 = xs[:].rearrange("p t c -> p (t c)")
        A = arena(free16, {"knT": (2, 512), "v": (4, 256), "qnT": (2, 256), "qrT": (256,),
                           "qr": (2, 2, 64), "ra": (2, 2, 32)})
        key2 = free8[:, 0:512].rearrange("p (t e c) -> p t e c", t=TT, e=2)
        krT = raw[:, 3, 0, :]
        prob = free8.rearrange("p (i k) -> p i k", i=4)
        probT = (modsb, hf)
        L = arena(free16, {"kst": (4, 96), "qst": (2, 96), "kT": (512,), "qT": (256,), "vst": (4, 194),
                           "vst_odd": (4, 194), "H": (2, 192), "negM": (2, 256), "mask": (2, P)})
        R = arena(free16, {"G": (2, 512), "M": (2, 512)})
        R2 = arena(free8, {"li": (2, 512), "lf": (2, 512)})
        wts = [flat.rearrange("p (d s t) -> p d s t", d=2, s=4)
               for flat in (free8, raw[:, 3].rearrange("p k c -> p (k c)"))]
        vst = [L["vst"], L["vst_odd"]]
        band = raw[:, 0].rearrange("p k c -> p (k c)").rearrange("p (s g t) -> p s g t", s=2, g=4)
        poolw = raw[:, 1].rearrange("p k c -> p (k c)").rearrange("p (g c d) -> p g c d", g=4, c=2)
        gateR = modsb[0:32, 0:P]
        gate_rows = kept[:, KEPT_AT["mv"] + 2 * D:KEPT_AT["mv"] + 3 * D]
        fw = free16[:, 0:D]
        poolT = kept[:, KEPT_AT["mv"]:KEPT_AT["mv"] + 8 * S].rearrange("p (i t) -> p i t", i=8)
        psum = stack.enter_context(nc.psum_tensor("psum", [P, 8, W], F32))
        TR, MOD = psum[:, TR_BANK, :], psum[:, MOD_BANK, :]

        def place_of(name, col, width, pair, pr):
            if pr is IN:
                return kv[name][:, 2 * pair:2 * pair + 2, col:col + width]
            base = KEPT_AT["mv"] + col * 2
            return kept[:, base:base + 2 * width].rearrange("p (t c) -> p t c", t=2)

        def y_tile(n):
            return place_of("y", n * W, W, 0, OUT)

        def banks(q):
            return 2 * (q % PAIR_BANKS)

        gates_landed = sem("gates_landed")
        par_in, x_in, xs_in = sem("par_in"), sem("x_in"), sem("xs_in")
        landed = {IN: [sem(f"landed{i}") for i in range(RAW)], OUT: [sem(f"out_landed{i}") for i in range(RAW)]}
        eps_set, par_turned, par_ready, c_ready = sem("eps_set"), sem("par_turned"), sem("par_ready"), sem("c_ready")
        sq_done, rms_root, rstd_ready = sem("sq_done"), sem("rms_root"), sem("rstd_ready")
        mod_zero = sem("mod_zero")
        xs_ready = sem("xs_ready")
        hi_done, lo_done, chunk_used = sem("hi_done"), sem("lo_done"), sem("chunk_used")
        mod_used, mod_copied = sem("mod_used"), sem("mod_copied")
        tr_filled, tr_read, vec_ready, scale_tmp = sem("tr_filled"), sem("tr_read"), sem("vec_ready"), sem("scale_tmp")
        hiT_done, full_done, loT_done = sem("hiT_done"), sem("full_done"), sem("loT_done")
        added = sem("added")
        cq_sq, cq_step, cq_root, cq_rstd, cq_scaled = sem("cq_sq"), sem("cq_step"), sem("cq_root"), sem("cq_rstd"), sem("cq_scaled")
        lat_turned, lat_hi, lat_full, lat_lo = sem("lat_turned"), sem("lat_hi"), sem("lat_full"), sem("lat_lo")
        silu_done, kr_tmp, kr_roped, kr_turned, krT_ready = (
            sem("silu_done"), sem("kr_tmp"), sem("kr_roped"), sem("kr_turned"), sem("krT_ready"))
        q_tmp, q_roped, qr_turned = sem("q_tmp"), sem("q_roped"), sem("qr_turned")
        kn_filled, qn_copied, qrT_copied, kn_copied, v_copied = (
            sem("kn_filled"), sem("qn_copied"), sem("qrT_copied"), sem("kn_copied"), sem("v_copied"))
        s_filled, max_done, negm_ready, p_ready = sem("s_filled"), sem("max_done"), sem("negm_ready"), sem("p_ready")
        p_turned, pT_ready, o_filled, rinv_ready, o_stored = (
            sem("p_turned"), sem("pT_ready"), sem("o_filled"), sem("rinv_ready"), sem("o_stored"))
        g_turned, g_step, gabs, g_exp, g_ln, em_in = (
            sem("g_turned"), sem("g_step"), sem("gabs"), sem("g_exp"), sem("g_ln"), sem("em_in"))
        gt_turned, gt_ready, et_ready, mask_in = sem("gt_turned"), sem("gt_ready"), sem("et_ready"), sem("mask_in")
        staged, picked, e_picked, ml_turned, ml_copied, sT_filled = (
            sem("staged"), sem("picked"), sem("e_picked"), sem("ml_turned"), sem("ml_copied"), sem("sT_filled"))
        arg_done, w_exp, w_mul, w_ready, h_filled = (
            sem("arg_done"), sem("w_exp"), sem("w_mul"), sem("w_ready"), sem("h_filled"))
        h_step, h_ready, h_sq, h_kept, ml_root, ml_rstd, ml_mixed = (
            sem("h_step"), sem("h_ready"), sem("h_sq"), sem("h_kept"), sem("ml_root"), sem("ml_rstd"), sem("ml_mixed"))
        pooled, pooled_copied, pool_filled, pool_mixed = (
            sem("pooled"), sem("pooled_copied"), sem("pool_filled"), sem("pool_mixed"))
        gate_turned, gate_row, gate_filled, gate_kept = (
            sem("gate_turned"), sem("gate_row"), sem("gate_filled"), sem("gate_kept"))
        xe_in, fw_in, e_scaled, e_summed, last_step, e_weighted = (
            sem("xe_in"), sem("fw_in"), sem("e_scaled"), sem("e_summed"), sem("last_step"), sem("e_weighted"))
        e_sq, e_root, e_rstd, act_out, dve_out, out_done = (
            sem("e_sq"), sem("e_root"), sem("e_rstd"), sem("act_out"), sem("dve_out"), sem("out_done"))

        block = stack.enter_context(nc.Block())

        def groups(engine, pr, run):
            run(pr, 0, 0, True, False)
            with engine.Fori(0, (NG - 2) // 2) as it:
                run(pr, it * 2 + 1, 1, False, False)
                run(pr, it * 2 + 2, 0, False, False)
            run(pr, NG - 1, 1, False, True)

        def pairs(engine, pair):
            with engine.Fori(0, PAIRS - 1) as hp:
                pair(hp, False)
            pair(PAIRS - 1, True)

        def heads(engine, step, peeled):
            step(0, 0)
            with engine.Fori(0, (MLH - 2 - peeled) // 2) as it:
                step(it * 2 + 1, 1)
                step(it * 2 + 2, 0)
            for h in range(MLH - 1 - peeled, MLH - 1):
                step(h, h % 2)

        @block.sync
        def _(sp):
            def load_mod(slot, kind, kc, g):
                src = w_mod[0, kc * KT * P:(kc + 1) * KT * P, bass.ds(g * W + kind * D, W)]
                sp.dma_start(raw[:, slot], src.rearrange("(k p) n -> p k n", p=P)).then_inc(landed[IN][slot], 16)

            def load_xs(g):
                for n, t in enumerate((x[0], ctx[0])):
                    src = t[:, bass.ds(g * W, W)].rearrange("(t p) n -> p t n", p=P)
                    sp.dma_start(xs[:, 2 * n:2 * n + 2, :], src).then_inc(xs_in, 16)

            def alone(pr, idx, last):
                if pr is not IN or not 0 < idx < len(pr.order[last]):
                    return False
                item = pr.order[last][idx]
                if item[0] == "w" and pr.tiles[item[1]][2] == 0:
                    assert idx == 2
                    return True
                return False

            def group(pr, g, buf, first, last):
                weight = w_in[0] if pr is IN else w_out[0]
                for idx, item in enumerate(pr.order[last]):
                    if pr is IN and idx == 6 and not last:
                        sp.wait_ge(tr_filled, g * pr.ntr + pr.tr0)
                        load_xs(g + 1)
                    slot = pr.slot(idx)
                    if pr is OUT and first and idx == 1:
                        sp.wait_ge(h_filled, MLH + 1)
                    if pr is OUT and first and idx == 3:
                        sp.wait_ge(h_kept, MLH + 1)
                        src = final_norm_w.rearrange("(a n) -> a n", a=1).to_broadcast([P, D])
                        sp.dma_start(fw, src).then_inc(fw_in, 16)
                    if pr is OUT and last and idx in (1, 3):
                        sp.wait_ge(xs_ready, TT * NG + NG)
                        t = idx // 2
                        sp.dma_start(kv["z"][:, t, :], x[0, t * P:(t + 1) * P, :]).then_inc(xe_in, 16)
                    if pr is OUT and first and idx == 2:
                        sp.wait_ge(pool_mixed, 8)
                    if pr is IN and first and idx < RAW:
                        sp.wait_ge(mod_used, PRO_MODS + idx - RAW + 1)
                    else:
                        if not alone(pr, idx, last) or first:
                            early = alone(pr, idx + 1, last) and not first
                            split, count = pr.free(idx + early, g, first) or (None, None)
                            assert not early or pr.free(idx, g, first)[0] == split
                            if split is not None:
                                sp.wait_ge(lo_done if split else mod_used, count)
                    if item[0] == "m":
                        load_mod(slot, item[1], item[2], g if item[1] == GATE else g + 1)
                        continue
                    name, _, col, width = pr.tiles[item[1]]
                    rows = weight[bass.ds(g * W, W), :]
                    dst = raw[:, slot, :, 0:width]
                    if name == "kg":
                        for at, n, col, there in ((0, 64, C_KR, landed[pr][slot]), (64, 32, C_GATES, gates_landed)):
                            src = rows[:, col:col + n].rearrange("(k p) n -> p k n", p=P)
                            sp.dma_start(dst[:, :, at:at + n], src).then_inc(there, 16)
                    else:
                        src = rows[:, col:col + width].rearrange("(k p) n -> p k n", p=P)
                        sp.dma_start(dst, src).then_inc(landed[pr][slot], 16)

            for kind in (SHIFT, SCALE):
                for kc in range(8):
                    n = 8 * kind + kc
                    if n >= RAW:
                        sp.wait_ge(mod_used, n - RAW + 1)
                    load_mod(n % RAW, kind, kc, 0)
            groups(sp, IN, group)

            with sp.Fori(0, PAIRS) as hp:
                for t in range(3):
                    sp.wait_ge(lo_done, hp * MLA_CHUNKS + (IN_CHUNKS - MLA_CHUNKS + KT * (t + 1)))
                    if t < 2:
                        src = w_uq[0, t * W:(t + 1) * W, bass.ds(hp * 384, 384)]
                        dst = raw[:, t, :, 0:384]
                    else:
                        src = w_ukv[0, :, bass.ds(hp * 512, 512)]
                        dst = raw[:, t]
                    sp.dma_start(dst, src.rearrange("(k p) n -> p k n", p=P)).then_inc(landed[IN][t], 16)

            sp.wait_ge(o_stored, 4 * PAIRS + 1)
            sp.dma_start(L["mask"], masks.rearrange("p (d t) -> p d t", d=2)).then_inc(mask_in, 16)
            sp.wait_ge(lo_done, OUT.chunk0)
            sp.dma_start(raw[:, 0].rearrange("p k c -> p (k c)"), bands).then_inc(landed[OUT][0], 16)
            src = pool_w[0].rearrange("g (c p) d -> p (g c) d", p=P)
            sp.dma_start(raw[:, 1].rearrange("p k (b c) -> p (k b) c", b=2), src).then_inc(landed[OUT][1], 16)
            groups(sp, OUT, group)

            for t in range(2):
                for there, n0, n1 in ((act_out, 0, Y_ACT), (dve_out, Y_ACT, OUT.n)):
                    sp.wait_ge(there, (t + 1) * (n1 - n0))
                    src = kept[:, KEPT_AT["mv"] + n0 * 2 * W:KEPT_AT["mv"] + n1 * 2 * W]
                    src = src.rearrange("p (n t c) -> p n t c", n=n1 - n0, t=2)[:, :, t, :]
                    dst = out[0, t * P:(t + 1) * P, n0 * W:n1 * W].rearrange("p (n c) -> p n c", n=n1 - n0)
                    sp.dma_start(dst, src).then_inc(out_done, 16)
            sp.wait_ge(out_done, 16 * 4)

        @block.gpsimd
        def _(pool):
            def scale_xs(g):
                if isinstance(g, int) and g == 0:
                    pool.wait_ge(x_in, 16 * TT)
                else:
                    pool.wait_ge(xs_in, g * 32)
                for t in range(TT):
                    src = xfull[:, t, 0:W] if isinstance(g, int) and g == 0 else xs[:, t, :]
                    nc.gpsimd.tensor_tensor(xs[:, t, :], src, rstd[:, t:t + 1].to_broadcast([P, W]),
                                            ALU.mult).then_inc(xs_ready, 1)

            def stage_mix(g):
                if not isinstance(g, int) or g > 0:
                    pool.wait_ge(tr_filled, g * OUT.ntr + IN_TR)
                nc.gpsimd.tensor_copy(xs[:, 0:2, :], kv["z"][:, :, bass.ds(g * W, W)]).then_inc(xs_ready, 1)

            pool.wait_ge(rstd_ready, 1)
            scale_xs(0)
            with pool.Fori(1, NG) as g:
                scale_xs(g)

            pool.wait_ge(et_ready, 1)
            for v in vst:
                nc.gpsimd.memset(v[:, :, MLV:MLV + 1], 1.0).then_inc(staged, 1)
            pool.wait_ge(staged, 2)

            def stage_head(h):
                pool.wait_ge(ml_turned, h + 1)
                nc.gpsimd.tensor_copy(L["kst"], kv["mk"][:, :, bass.ds(h * DQK, DQK)]).then_inc(staged, 1)
                nc.gpsimd.tensor_copy(L["qst"], kv["mq"][:, :, bass.ds(h * DQK, DQK)]).then_inc(staged, 1)

            def strike(h, par):
                for d in range(2):
                    pool.wait_ge(w_mul, h * 2 + d + 2)
                    w = wts[par][:, d, 2:4, :].rearrange("p s (a c) -> p (s a) c", a=2)[:, ::3, :]
                    nc.gpsimd.tensor_tensor(w, w, L["mask"][:, d:d + 1].to_broadcast([P, 2, P]), ALU.mult).then_inc(w_ready, 1)

            def head_step(h, par):
                stage_head(h + 1)
                strike(h, par)

            stage_head(0)
            pool.wait_ge(mask_in, 16)
            heads(pool, head_step, 0)
            strike(MLH - 1, 1)
            pool.wait_ge(h_filled, MLH)
            pool.wait_ge(o_stored, 4 * PAIRS + 1)
            stage_mix(0)
            with pool.Fori(1, AT_ML // W) as g:
                stage_mix(g)
            pool.wait_ge(ml_mixed, 2 * MLH)
            pool.wait_ge(pool_mixed, 8)
            with pool.Fori(AT_ML // W, NG) as g:
                stage_mix(g)

            pool.wait_ge(xe_in, 32)
            for n in range(Y_POOL):
                pool.wait_ge(added, IN_PAIRS + OUT.npairs * (NG - 1) + n + 1)
                pool.wait_ge(gate_kept, n + 1)
                gate = gate_rows[:, n * W:(n + 1) * W].unsqueeze(1).to_broadcast([P, 2, W])
                nc.gpsimd.tensor_tensor(y_tile(n), y_tile(n), gate, ALU.mult).then_inc(e_scaled, 1)
                pool.wait_ge(e_scaled, n + 1)
                nc.gpsimd.tensor_tensor(y_tile(n), y_tile(n), kv["z"][:, :, n * W:(n + 1) * W],
                                        ALU.add).then_inc(e_summed, 1)

        @block.scalar
        def _(act):
            for s in (p_ready, h_sq):
                act.sem_inc(s, 1)
            act.dma_start(tab[:], tables).then_inc(par_in, 16)
            act.dma_start(par_rows[0:96, 0], b_mod[0].rearrange("(a n) -> a n", n=P)).then_inc(par_in, 16)
            act.dma_start(par_rows[96:128, 0], norm_w[0].rearrange("(a n) -> a n", n=P)).then_inc(par_in, 16)
            rows = 0
            for src in (c[0], c_ctx, q_norm_w[0], kv_norm_w[0], ml_norm_w[0], pool_scale[0]):
                n = src.shape[0] // P
                act.dma_start(par_rows[rows:rows + n, 1], src.rearrange("(a n) -> a n", n=P)).then_inc(par_in, 16)
                rows += n
            for n, src in enumerate((ml_b_i[0, 0], ml_b_i[0, 1], ml_b_f[0, 0], ml_b_f[0, 1])):
                act.dma_start(bif[:, n:n + 1], src.rearrange("(h o) -> h o", o=1)).then_inc(par_in, 16)
            for t in range(TT):
                src = (x, ctx)[t // 2][0, (t % 2) * P:(t % 2 + 1) * P, :]
                act.dma_start(xfull[:, t, :], src).then_inc(x_in, 16)
            act.wait_ge(par_ready, 2)
            nc.scalar.activation(cT[:].rearrange("p a k -> p (a k)"), par2[:, 0:64], ACT.Silu).then_inc(c_ready, 1)
            act.wait_ge(x_in, 16 * TT)
            for t in range(TT):
                if t > 0:
                    act.wait_ge(sq_done, t)
                nc.scalar.activation(kept[:, TT * D:(TT + 1) * D], xfull[:, t, :], ACT.Square,
                                     accum_out=sums[:, t:t + 1]).then_inc(sq_done, 1)
            act.wait_ge(eps_set, 2)
            act.wait_ge(sq_done, TT)
            nc.scalar.activation(rstd[:, 0:4], sums[:, 0:4], ACT.Sqrt, bias=epst[:, 0:1], scale=1.0 / D).then_inc(rms_root, 1)

            def copy_mod(n, before):
                act.wait_ge(tr_filled, before)
                act.wait_ge(mod_used, n * 8 + 8)
                nc.scalar.copy(modsb[:], MOD).then_inc(mod_copied, 1)

            def turn(pr, g, buf, k, use, vecs, bank=TR_BANK):
                src = psum[:, bank, :]
                act.wait_ge(tr_filled, use + 1)
                if k == 0:
                    act.wait_ge(vec_ready, vecs)
                for i in range(2 if pr is IN else 1):
                    seg = slice(i * S, (i + 1) * S)
                    dst = hT[:, buf, 0, k, seg]
                    if pr is IN:
                        a = nc.scalar.activation(dst, src[:, seg], ACT.Identity, bias=shiftv[:, k, i:i + 1],
                                                 scale=scalev[:, k, i:i + 1])
                    else:
                        a = nc.scalar.activation(dst, src[:, seg], ACT.Copy, scale=scalev[:, k, 0:1])
                a.then_inc(hiT_done, 1)

            def split(pr, slot, j, k, g, width):
                place = (KT * j + k) % PART
                if pr is not IN or not (isinstance(g, int) and g == 0 and KT * j + k < PART):
                    act.wait_ge(chunk_used, pr.chunk(j, k, g) - PART)
                nc.scalar.copy(part[:, place, 0, 0:width], raw[:, slot, k, 0:width]).then_inc(hi_done, 1)

            def y_squares(n):
                if n < Y_POOL:
                    act.wait_ge(e_summed, n + 1)
                else:
                    act.wait_ge(last_step, 2)
                for t in range(2):
                    if n + t > 0:
                        act.wait_ge(e_sq, 2 * n + t)
                    nc.scalar.activation(hf[:], y_tile(n)[:, t, :], ACT.Square, accum_out=rall[:, n, t:t + 1]).then_inc(e_sq, 1)

            def keep_gate(n):
                act.wait_ge(gate_filled, n + 1)
                nc.scalar.copy(gate_rows[:, n * W:(n + 1) * W], psum[:, MOD_BANK + n % 2, :]).then_inc(gate_kept, 1)

            def rank_squares(n):
                if n == 0:
                    act.wait_ge(added, RANKS_SUMMED)
                    act.wait_ge(loT_done, KT * NG)
                else:
                    act.wait_ge(cq_sq, n)
                if n < 4:
                    src, at = kv["ckv"][:, n, :], 2 + n
                else:
                    src, at = kv["cq"][:, n % 2, (n // 6) * W:(n // 6 + 1) * W], n % 2 + 6 * (n // 6)
                nc.scalar.activation(hf[:], src, ACT.Square, accum_out=sums[:, at:at + 1]).then_inc(cq_sq, 1)

            def rank_roots():
                act.wait_ge(cq_step, 1)
                act.wait_ge(xs_ready, TT * NG)
                nc.scalar.activation(rstd[:, 0:2], sums[:, 0:2], ACT.Sqrt, bias=epst[:, 0:1], scale=1.0 / Q_RANK).then_inc(cq_root, 1)
                nc.scalar.activation(rstd[:, 2:6], sums[:, 2:6], ACT.Sqrt, bias=epst[:, 0:1], scale=1.0 / KV_RANK).then_inc(cq_root, 1)

            def gate_tile(j):
                name, col, _, width = IN.tiles[j]
                if name in ("z", "mo"):
                    act.wait_ge(added, summed(j))
                    y = place_of(name, col, width, 0, IN)
                    nc.scalar.activation(y, y, ACT.Silu if name == "z" else ACT.Sigmoid).then_inc(silu_done, 1)

            def beside_last(j):
                if 6 <= j <= 9:
                    rank_squares(2 * j - 12)
                    rank_squares(2 * j - 11)
                if j == 12:
                    rank_roots()
                if j >= LAST_Z:
                    gate_tile(j - LAST_Z)

            def group(pr, g, buf, first, last):
                _, copies, others = turn_events(pr, last)
                for idx, item in enumerate(pr.order[last]):
                    if item[0] == "m":
                        continue
                    j = item[1]
                    slot = pr.slot(idx)
                    if pr is OUT and last:
                        if j == 0:
                            act.wait_ge(ml_mixed, 2 * MLH)
                        if 2 <= j <= 5:
                            keep_gate(2 * j - 4)
                            keep_gate(2 * j - 3)
                        if j >= 4:
                            y_squares(j - 4)
                    act.wait_ge(landed[pr][slot], pr.landed_at(idx, g))
                    if pr.tiles[j][0] == "kg":
                        act.wait_ge(gates_landed, g * 16 + 16)
                    for k in range(KT):
                        split(pr, slot, j, k, g, pr.tiles[j][3])
                    if pr is IN and last:
                        beside_last(j)
                    if j in copies:
                        kind = 0 if last else {8: 0, 16: 1, pr.n - 1: 2}[j]
                        copy_mod(g * 3 + (2 + kind), g * pr.ntr + (pr.tr0 + kind))
                    for what, number, use in others.get(j, ()):
                        if what == "turn":
                            vecs = g * 3 + 4 if pr is IN else g + (IN_VECS + 2)
                            turn(pr, g + 1, 1 - buf, number, g * pr.ntr + (pr.tr0 + use), vecs)

            copy_mod(0, 2)
            copy_mod(1, 3)
            for k in range(KT):
                turn(IN, 0, 0, k, 4 + k, 2, bank=k)
            groups(act, IN, group)

            act.wait_ge(kr_turned, 1)
            act.wait_ge(lo_done, IN_CHUNKS)
            nc.scalar.copy(krT, psum[:, 7, :]).then_inc(krT_ready, 1)

            def turned_rank(n):
                act.wait_ge(lat_turned, n + 1)
                for i in range(2 if n < 4 else 1):
                    w = par2[:, 64 + 2 * n + i:65 + 2 * n + i] if n < 4 else par2[:, 72 + n - 4:73 + n - 4]
                    width = S if n < 4 else TT * P
                    seg = slice(i * width, (i + 1) * width)
                    dst = hT[:, 0, 0, n, seg] if n < 4 else hT[:, 1, 0, n - 4, :]
                    a = nc.scalar.activation(dst, psum[:, n, seg], ACT.Copy, scale=w)
                a.then_inc(lat_hi, 1)

            def split_up(hp, n):
                if n % KT == 0:
                    act.wait_ge(landed[IN][n // KT], hp * 16 + 16 * (IN_RAW // RAW + 1))
                width = 384 if n < 8 else 512
                act.wait_ge(chunk_used, hp * MLA_CHUNKS + (IN_CHUNKS + n + 1 - PART))
                nc.scalar.copy(part[:, n % PART, 0, 0:width], raw[:, n // KT, n % KT, 0:width]).then_inc(hi_done, 1)

            def pair(hp, last):
                for n in range(PART, MLA_CHUNKS):
                    split_up(hp, n)
                act.wait_ge(chunk_used, hp * MLA_CHUNKS + (IN_CHUNKS + 8))
                act.wait_ge(s_filled, hp * 4 + 1)
                nc.scalar.copy(A["qnT"], psum[:, 0:2, 0:S]).then_inc(qn_copied, 1)
                act.wait_ge(kn_filled, hp + 1)
                nc.scalar.copy(A["knT"], psum[:, 4:6, :]).then_inc(kn_copied, 1)
                act.wait_ge(qr_turned, hp + 2)
                nc.scalar.copy(A["qrT"], psum[:, 2, 0:S]).then_inc(qrT_copied, 1)
                for i in range(4):
                    act.wait_ge(negm_ready, hp * 4 + i + 1)
                    act.wait_ge(p_turned, hp * 4 + 1)
                    act.wait_ge(rinv_ready, hp * 4 + 1)
                    nc.scalar.activation(prob[:, i], psum[:, 2 + i, :], ACT.Exp, bias=negm[:, i:i + 1], scale=MLA_SCALE,
                                         accum_out=rows_s[:, i:i + 1]).then_inc(p_ready, 1)
                if not last:
                    for n in range(PART):
                        split_up(hp + 1, n)

            for n in range(4):
                turned_rank(n)
            for n in range(PART):
                split_up(0, n)
            for n in range(4, 8):
                turned_rank(n)
            for j in range(IN.n - LAST_Z, IN.n):
                gate_tile(j)
            pairs(act, pair)

            act.wait_ge(g_step, 1)
            nc.scalar.activation(R["G"][0:MLH], R2["lf"][0:MLH], ACT.Abs).then_inc(gabs, 1)
            act.wait_ge(gabs, 1)
            nc.scalar.activation(R["M"][0:MLH], R["G"][0:MLH], ACT.Exp, scale=-1.0).then_inc(g_exp, 1)
            act.wait_ge(g_exp, 1)
            nc.scalar.activation(R["G"][0:MLH], R["M"][0:MLH], ACT.Ln, bias=epst[0:MLH, 1:2]).then_inc(g_ln, 1)
            act.wait_ge(gt_turned, 1)
            nc.scalar.copy(Gt[:], psum[:, 4, 0:64].rearrange("p (a h) -> p a h", a=8)).then_inc(gt_ready, 1)
            nc.scalar.activation(Et[:], psum[:, 4, 64:96].rearrange("p (a h) -> p a h", a=4), ACT.Exp).then_inc(et_ready, 1)
            def head_in(h, par):
                act.wait_ge(ml_turned, h + 2)
                nc.scalar.activation(L["kT"][0:DQK], psum[0:DQK, 0, :], ACT.Copy, scale=ML_SCALE).then_inc(ml_copied, 1)
                nc.scalar.copy(L["qT"][0:DQK], psum[0:DQK, 1, 0:S]).then_inc(ml_copied, 1)
                if not isinstance(h, int) or h > 1:
                    act.wait_ge(h_filled, h)
                nc.scalar.copy(vst[par][:, :, 0:MLV], kv["mv"][:, :, bass.ds(h * MLV, MLV)]).then_inc(ml_copied, 1)

            def weights(h, par):
                for d in range(2):
                    act.wait_ge(arg_done, h * 2 + d + 1)
                    nc.scalar.activation(wts[par][:, d], wts[par][:, d], ACT.Exp).then_inc(w_exp, 1)

            def squares(h):
                act.wait_ge(h_ready, h + 2)
                act.wait_ge(h_kept, h + 1)
                act.wait_ge(h_sq, h * 2 + 1)
                for t in range(2):
                    nc.scalar.activation(modsb[:, t * MLV:(t + 1) * MLV], L["H"][:, t, :], ACT.Square,
                                         accum_out=ssh[:, t:t + 1]).then_inc(h_sq, 1)

            def head_step(h, par):
                head_in(h + 1, 1 - par)
                if not isinstance(h, int) or h > 0:
                    squares(h - 1)
                weights(h + 1, 1 - par)

            act.wait_ge(et_ready, 1)
            head_in(0, 0)
            weights(0, 0)
            heads(act, head_step, 0)
            squares(MLH - 2)
            for k in range(KT):
                turn(OUT, 0, 0, k, IN_TR + k, IN_VECS + 1, bank=k)
            squares(MLH - 1)
            act.wait_ge(ml_copied, 3 * MLH)
            for i in range(8):
                act.wait_ge(pooled, i + 1)
                nc.scalar.copy(poolT[:, i, :], psum[:, 4 + i % 4, 0:S]).then_inc(pooled_copied, 1)
            act.wait_ge(h_kept, MLH + 1)
            nc.scalar.activation(rall[:], ssall[:], ACT.Sqrt, bias=epst[:, 0:1], scale=1.0 / MLV).then_inc(ml_root, 1)
            act.wait_ge(gate_turned, 1)
            act.wait_ge(h_sq, 2 * MLH + 1)
            nc.scalar.copy(gateR, psum[0:32, MOD_BANK, 0:P]).then_inc(gate_row, 1)
            groups(act, OUT, group)

            for n in range(OUT.n - 4, OUT.n):
                y_squares(n)
            act.wait_ge(e_rstd, 1)
            nc.scalar.activation(rstd[:, 0:2], sums[:, 0:2], ACT.Sqrt, bias=epst[:, 0:1], scale=1.0 / D).then_inc(e_root, 1)
            act.wait_ge(e_rstd, 2)
            act.wait_ge(e_weighted, Y_ACT)
            for t in range(2):
                for n in range(Y_ACT):
                    nc.scalar.activation(y_tile(n)[:, t, :], y_tile(n)[:, t, :], ACT.Copy,
                                         scale=rstd[:, t:t + 1]).then_inc(act_out, 1)

        @block.vector
        def _(dve):
            for s in (o_stored, rinv_ready, q_roped, pT_ready, h_kept, h_ready, w_mul):
                dve.sem_inc(s, 1)
            nc.vector.memset(epst[:, 0:1], EPS).then_inc(eps_set, 1)
            nc.vector.memset(epst[:, 1:2], 1.0).then_inc(eps_set, 1)
            nc.vector.memset(MOD, 0.0).then_inc(mod_zero, 1)
            nc.vector.memset(colsc[:, 0:AT_ML // P], 1.0).then_inc(eps_set, 1)
            dve.wait_ge(tr_filled, 1)
            nc.vector.tensor_copy(par1[:], TR[:, 0:P]).then_inc(par_ready, 1)
            dve.wait_ge(par_ready, 1)
            nc.vector.tensor_scalar(par1[:, 32:64], par1[:, 32:64], 1.0, None, ALU.add).then_inc(tr_read, 1)
            dve.wait_ge(tr_filled, 2)
            nc.vector.tensor_copy(par2[:], TR[:, 0:96]).then_inc(par_ready, 1)
            dve.wait_ge(par_ready, 2)
            dve.wait_ge(tr_read, 1)
            nc.vector.tensor_copy(colsc[:, AT_ML // P:32], par2[:, 76:96]).then_inc(tr_read, 1)
            dve.wait_ge(rms_root, 1)
            nc.vector.memset(place_of("z", D - W, W, 0, IN), 0.0).then_inc(eps_set, 1)
            nc.vector.reciprocal(rstd[:, 0:4], rstd[:, 0:4]).then_inc(rstd_ready, 1)

            def vec(kind, g, use, vecs):
                src = TR[:, 0:8].rearrange("p (k j) -> p k j", j=2)
                dve.wait_ge(tr_filled, use + 1)
                if kind == GATE:
                    nc.vector.tensor_tensor(gateK[:, bass.ds(g * KT, KT)], src[:, :, 0], par1[:, bass.ds(g * KT + 64, KT)],
                                            ALU.add).then_inc(vec_ready, 1)
                else:
                    base = 0 if kind == SHIFT else 32
                    bias = par1[:, bass.ds(g * KT + base, KT)].unsqueeze(2).to_broadcast([P, KT, 2])
                    if not isinstance(g, int) or g > 0:
                        dve.wait_ge(hiT_done, g * KT)
                        dve.wait_ge(full_done, g * KT)
                    if kind == SHIFT:
                        nc.vector.tensor_tensor(shiftv[:], src, bias, ALU.add).then_inc(vec_ready, 1)
                    else:
                        nc.vector.tensor_tensor(scalet[:], src, bias, ALU.add).then_inc(scale_tmp, 1)
                        dve.wait_ge(scale_tmp, g + 1)
                        w = par1[:, bass.ds(g * KT + 96, KT)].unsqueeze(2).to_broadcast([P, KT, 2])
                        nc.vector.tensor_tensor(scalev[:], scalet[:], w, ALU.mult).then_inc(vec_ready, 1)
                dve.wait_ge(vec_ready, vecs + 1)
                dve.sem_inc(tr_read, 1)

            def turn(pr, g, buf, k, use, count, bank=TR_BANK):
                src = psum[:, bank, :]
                dve.wait_ge(tr_filled, use + 1)
                dve.wait_ge(loT_done, count)
                dve.wait_ge(hiT_done, count + 1)
                for i in range(2 if pr is IN else 1):
                    seg = slice(i * S, (i + 1) * S)
                    if pr is IN:
                        a = nc.vector.tensor_scalar(hf[:, seg], src[:, seg], scalev[:, k, i:i + 1], shiftv[:, k, i:i + 1],
                                                    ALU.mult, ALU.add)
                    else:
                        a = nc.vector.tensor_scalar(hf[:, seg], src[:, seg], scalev[:, k, 0:1], None, ALU.mult)
                a.then_inc(full_done, 1)
                dve.wait_ge(full_done, count + 1)
                n = 2 * S if pr is IN else S
                nc.vector.tensor_tensor(hT[:, buf, 1, k, 0:n], hf[:, 0:n], hT[:, buf, 0, k, 0:n].bitcast(F32),
                                        ALU.subtract).then_inc(loT_done, 1)
                dve.wait_ge(loT_done, count + 1)
                dve.sem_inc(tr_read, 1)

            def lows(pr, slot, j, g, width):
                for k in range(KT):
                    place = (KT * j + k) % PART
                    dve.wait_ge(hi_done, pr.chunk(j, k, g))
                    nc.vector.tensor_tensor(part[:, place, 1, 0:width], raw[:, slot, k, 0:width],
                                            part[:, place, 0, 0:width].bitcast(F32), ALU.subtract).then_inc(lo_done, 1)

            def add(pr, j, g, first):
                name, col, _, width = pr.tiles[j]
                dve.wait_ge(chunk_used, pr.chunk(j, KT - 1, g))
                q0, n = pr.pair[j]
                for i in range(n):
                    b = banks(q0 + i)
                    dst = place_of(name, col, width, i, pr)
                    if first:
                        nc.vector.tensor_copy(dst, psum[:, b:b + 2, 0:width]).then_inc(added, 1)
                    else:
                        dve.wait_ge(added, g * pr.npairs + (pr.pair0 - pr.npairs + q0 + i + 1))
                        nc.vector.tensor_tensor(dst, dst, psum[:, b:b + 2, 0:width], ALU.add).then_inc(added, 1)

            def mix_mlstm(h):
                for t in range(2):
                    dst = kv["z"][:, t, AT_ML + h * MLV:AT_ML + (h + 1) * MLV]
                    nc.vector.scalar_tensor_tensor(out=dst, in0=kv["mo"][:, t, h * MLV:(h + 1) * MLV],
                                                   scalar=rall[:, h, t:t + 1], in1=dst, op0=ALU.mult,
                                                   op1=ALU.mult).then_inc(ml_mixed, 1)

            def rope_key():
                dve.wait_ge(added, KG_SUMMED)
                k1, k2 = kv["kg"][:, 0:2, 0:32], kv["kg"][:, 0:2, 32:64]
                tmp = hf[:, 0:256].rearrange("p (n t c) -> p n t c", n=4, t=2)
                for n, (a, b) in enumerate(((k1, cosv), (k2, sinv), (k1, sinv), (k2, cosv))):
                    nc.vector.tensor_tensor(tmp[:, n], a, b, ALU.mult).then_inc(kr_tmp, 1)
                dve.wait_ge(kr_tmp, 4)
                nc.vector.tensor_tensor(k1, tmp[:, 0], tmp[:, 1], ALU.subtract).then_inc(kr_roped, 1)
                nc.vector.tensor_tensor(k2, tmp[:, 2], tmp[:, 3], ALU.add).then_inc(kr_roped, 1)
                dve.wait_ge(kr_roped, 2)
                for e in range(2):
                    nc.vector.tensor_copy(key2[:, :, e, :], kv["kg"][:, :, 0:ROPE]).then_inc(kr_roped, 1)

            def scale_ranks(name, r):
                for t in range(KEPT[name][0]):
                    nc.vector.tensor_scalar(kv[name][:, t, :], kv[name][:, t, :], rstd[:, r + t:r + t + 1], None,
                                            ALU.mult).then_inc(cq_scaled, 1)

            def beside_last(j):
                if j == 11:
                    dve.wait_ge(cq_sq, 8)
                    nc.vector.tensor_tensor(sums[:, 0:2], sums[:, 0:2], sums[:, 6:8], ALU.add).then_inc(cq_step, 1)
                if j == 14:
                    dve.wait_ge(cq_root, 2)
                    nc.vector.reciprocal(rstd[:, 0:6], rstd[:, 0:6]).then_inc(cq_rstd, 1)
                    dve.wait_ge(cq_rstd, 1)
                    scale_ranks("cq", 0)
                if j == 15:
                    scale_ranks("ckv", 2)
                if j == IN.n - 1:
                    rope_key()

            def group(pr, g, buf, first, last):
                _, _, others = turn_events(pr, last)
                for idx, item in enumerate(pr.order[last]):
                    if item[0] == "m":
                        continue
                    j = item[1]
                    if pr is OUT and j == 1 and not last:
                        dve.wait_ge(hiT_done, g * KT + OUT.hT0)
                        dve.wait_ge(full_done, g * KT + OUT.hT0)
                        nc.vector.tensor_copy(scalev[:, :, 0], colsc[:, bass.ds(g * KT + KT, KT)]).then_inc(vec_ready, 1)
                        dve.wait_ge(vec_ready, g + IN_VECS + 2)
                    lows(pr, pr.slot(idx), j, g, pr.tiles[j][3])
                    if pr is OUT and first:
                        mix_mlstm(j)
                    if j > 0:
                        add(pr, j - 1, g, first)
                    elif not first:
                        add(pr, pr.n - 1, g - 1, False)
                        for what, number, use in turn_events(pr, False)[2].get(pr.n, ()):
                            vec(number, g - 1, g * pr.ntr + (pr.tr0 - pr.ntr + use), g * 3 + 1)
                    for what, number, use in others.get(j, ()):
                        if what == "turn":
                            turn(pr, g + 1, 1 - buf, number, g * pr.ntr + (pr.tr0 + use), g * KT + (pr.hT0 + number))
                        elif number == GATE:
                            vec(GATE, g, g * pr.ntr + (pr.tr0 + use), g * 3 + 2)
                        else:
                            vec(number, g + 1, g * pr.ntr + (pr.tr0 + use), g * 3 + (2 + number))
                    if pr is IN and last:
                        beside_last(j)
                    if pr is OUT and last and j >= OUT.n - Y_ACT:
                        n = j - (OUT.n - Y_ACT)
                        dve.wait_ge(fw_in, 16)
                        dve.wait_ge(e_sq, 2 * n + 2)
                        w = fw[:, n * W:(n + 1) * W].unsqueeze(1).to_broadcast([P, 2, W])
                        nc.vector.tensor_tensor(y_tile(n), y_tile(n), w, ALU.mult).then_inc(e_weighted, 1)
                if last:
                    add(pr, pr.n - 1, g, False)

            vec(SHIFT, 0, 2, 0)
            vec(SCALE, 0, 3, 1)
            for k in range(KT):
                turn(IN, 0, 0, k, 4 + k, k, bank=k)
            dve.wait_ge(eps_set, 4)
            groups(dve, IN, group)

            def turned_rank(n):
                dve.wait_ge(lat_turned, n + 1)
                dve.wait_ge(lat_lo, n)
                dve.wait_ge(lat_hi, n + 1)
                for i in range(2 if n < 4 else 1):
                    w = par2[:, 64 + 2 * n + i:65 + 2 * n + i] if n < 4 else par2[:, 72 + n - 4:73 + n - 4]
                    width = S if n < 4 else TT * P
                    seg = slice(i * width, (i + 1) * width)
                    a = nc.vector.tensor_scalar(hf[:, seg], psum[:, n, seg], w, None, ALU.mult)
                a.then_inc(lat_full, 1)
                dve.wait_ge(lat_full, n + 1)
                b, k = (0, n) if n < 4 else (1, n - 4)
                nc.vector.tensor_tensor(hT[:, b, 1, k, :], hf[:], hT[:, b, 0, k, :].bitcast(F32),
                                        ALU.subtract).then_inc(lat_lo, 1)

            def low_part(hp, n):
                width = 384 if n < 8 else 512
                dve.wait_ge(hi_done, hp * MLA_CHUNKS + (IN_CHUNKS + n + 1))
                nc.vector.tensor_tensor(part[:, n % PART, 1, 0:width], raw[:, n // KT, n % KT, 0:width],
                                        part[:, n % PART, 0, 0:width].bitcast(F32), ALU.subtract).then_inc(lo_done, 1)

            def pair(hp, last):
                for n in range(PART, MLA_CHUNKS):
                    low_part(hp, n)
                dve.wait_ge(chunk_used, hp * MLA_CHUNKS + (IN_CHUNKS + 8))
                dve.wait_ge(qr_turned, hp + 1)
                q = psum[:, 2:4, 0:2 * ROPE].rearrange("p t (e c) -> p t e c", e=2)
                cb = cosv.unsqueeze(2).to_broadcast([P, 2, 2, 32])
                sb_ = sinv.unsqueeze(2).to_broadcast([P, 2, 2, 32])
                r1, r2, ra = A["qr"][:, :, :, 0:32], A["qr"][:, :, :, 32:64], A["ra"]
                nc.vector.tensor_tensor(r1, q[:, :, :, 0:32], cb, ALU.mult).then_inc(q_tmp, 1)
                nc.vector.tensor_tensor(r2, q[:, :, :, 0:32], sb_, ALU.mult).then_inc(q_tmp, 1)
                dve.wait_ge(q_roped, hp * 2 + 1)
                nc.vector.tensor_tensor(ra, q[:, :, :, 32:64], sb_, ALU.mult).then_inc(q_tmp, 1)
                dve.wait_ge(q_tmp, hp * 4 + 3)
                nc.vector.tensor_tensor(r1, r1, ra, ALU.subtract).then_inc(q_roped, 1)
                dve.wait_ge(q_roped, hp * 2 + 2)
                nc.vector.tensor_tensor(ra, q[:, :, :, 32:64], cb, ALU.mult).then_inc(q_tmp, 1)
                dve.wait_ge(q_tmp, hp * 4 + 4)
                nc.vector.tensor_tensor(r2, r2, ra, ALU.add).then_inc(q_roped, 1)
                dve.wait_ge(chunk_used, hp * MLA_CHUNKS + (IN_CHUNKS + 12))
                dve.wait_ge(o_filled, hp * 4 + 1)
                nc.vector.tensor_copy(A["v"][:, 0:2], psum[:, 6:8, 0:2 * DV]).then_inc(v_copied, 1)
                nc.vector.tensor_copy(A["v"][:, 2:4], psum[:, 0:2, 0:2 * DV]).then_inc(v_copied, 1)
                for i in range(4):
                    dve.wait_ge(s_filled, hp * 4 + i + 2)
                    dve.wait_ge(p_ready, hp * 4 + 1)
                    nc.vector.tensor_reduce(negm[:, i:i + 1], psum[:, 2 + i, :], AX_X, ALU.max, negate=True).then_inc(max_done, 1)
                    dve.wait_ge(max_done, hp * 4 + i + 1)
                    nc.vector.tensor_scalar(negm[:, i:i + 1], negm[:, i:i + 1], MLA_SCALE, None, ALU.mult).then_inc(negm_ready, 1)

                def probs_out(i):
                    dve.wait_ge(p_turned, hp * 4 + i + 2)
                    dve.wait_ge(o_filled, hp * 4 + max(i - 1, 0) + 1)
                    nc.vector.tensor_copy(probT[i % 2][:], psum[:, 6 + i % 2, :]).then_inc(pT_ready, 1)

                def head_out(i):
                    dve.wait_ge(p_ready, hp * 4 + i + 2)
                    dve.wait_ge(o_stored, hp * 4 + 1)
                    nc.vector.reciprocal(rinv[:, i:i + 1], rows_s[:, i:i + 1]).then_inc(rinv_ready, 1)
                    dve.wait_ge(rinv_ready, hp * 4 + i + 2)
                    dve.wait_ge(o_filled, hp * 4 + i + 2)
                    dst = kv["z"][:, i // 2, bass.ds(hp * (2 * DV) + (i % 2) * DV, DV)]
                    nc.vector.scalar_tensor_tensor(out=dst, in0=psum[:, i % 2, 0:DV], scalar=rinv[:, i:i + 1], in1=dst,
                                                   op0=ALU.mult, op1=ALU.mult).then_inc(o_stored, 1)

                probs_out(0)
                probs_out(1)
                head_out(0)
                probs_out(2)
                head_out(1)
                probs_out(3)
                if not last:
                    for n in range(PART):
                        low_part(hp + 1, n)
                head_out(2)
                head_out(3)

            for n in range(4):
                turned_rank(n)
            for n in range(PART):
                low_part(0, n)
            for n in range(4, 8):
                turned_rank(n)
            dve.wait_ge(silu_done, GATED)
            pairs(dve, pair)

            li, lf, G, M = R2["li"][0:MLH], R2["lf"][0:MLH], R["G"][0:MLH], R["M"][0:MLH]
            ones = hf[0:MLH, :]
            steps = [0]

            def step(instruction):
                instruction.then_inc(g_step, 1)
                steps[0] += 1

            dve.wait_ge(g_turned, 1)
            dve.wait_ge(p_turned, 4 * PAIRS + 1)
            for d in range(2):
                nc.vector.tensor_scalar(li[:, d, :], psum[0:MLH, 2 + d, :], bif[:, d:d + 1], None, ALU.add)
            nc.vector.tensor_scalar(lf[:, 0, :], psum[0:MLH, 4, :], bif[:, 2:3], None, ALU.add)
            step(nc.vector.tensor_scalar(lf[:, 1, :], psum[0:MLH, 5, :], bif[:, 3:4], None, ALU.add))
            step(nc.vector.memset(ones, 1.0))
            dve.wait_ge(g_ln, 1)
            dve.wait_ge(g_step, 2)
            step(nc.vector.scalar_tensor_tensor(out=lf, in0=lf, scalar=0.0, in1=G, op0=ALU.min, op1=ALU.subtract))
            dve.wait_ge(g_step, 3)

            def runs(dst, src0, src1, op0, op1, start):
                step(nc.vector.tensor_tensor_scan(dst[:, 0, :], src0(0, slice(0, 512), False), src1[:, 0, :], start, op0, op1))
                step(nc.vector.tensor_tensor_scan(dst[:, 1, 0:S][:, ::-1], src0(1, slice(0, S), True),
                                                  src1[:, 1, 0:S][:, ::-1], start, op0, op1))
                dve.wait_ge(g_step, steps[0])
                step(nc.vector.tensor_tensor_scan(dst[:, 1, S:2 * S][:, ::-1], src0(1, slice(S, 2 * S), True),
                                                  src1[:, 1, S:2 * S][:, ::-1], dst[:, 1, 0:1], op0, op1))
                dve.wait_ge(g_step, steps[0])

            runs(M, lambda d, seg, back: ones[:, 0:seg.stop - seg.start], lf, ALU.mult, ALU.add, 0.0)
            step(nc.vector.tensor_tensor(G, li, M, ALU.subtract))
            dve.wait_ge(g_step, steps[0])
            runs(lf, lambda d, seg, back: G[:, d, seg][:, ::-1] if back else G[:, d, seg], G, ALU.max, ALU.max, 0.0)
            step(nc.vector.tensor_scalar(L["negM"][0:MLH], lf[:, :, S:2 * S], -1.0, None, ALU.mult))
            dve.wait_ge(g_step, steps[0])
            step(nc.vector.tensor_tensor(li[:, :, S:2 * S], L["negM"][0:MLH], M[:, :, S:2 * S], ALU.subtract))
            assert steps[0] == G_STEPS

            dve.wait_ge(gt_ready, 1)
            dve.wait_ge(et_ready, 1)

            def pick(h):
                dve.wait_ge(ml_turned, h + 1)
                if not isinstance(h, int) or h > 0:
                    dve.wait_ge(arg_done, h * 2)
                nc.vector.tensor_copy(selh[:], ident[0:MLH, bass.ds(h, 1)].to_broadcast([MLH, P])).then_inc(picked, 1)
                nc.vector.tensor_copy(Gh[:].unsqueeze(2), Gt[:, :, bass.ds(h, 1)]).then_inc(picked, 1)

            def exponents(h, par):
                dve.wait_ge(picked, h * 2 + 2)
                dve.wait_ge(ml_turned, h + 2)
                if not isinstance(h, int) or h > 1:
                    dve.wait_ge(h_filled, h)
                for d in range(2):
                    for s in range(4):
                        a = nc.vector.tensor_scalar(wts[par][:, d, s, :], psum[:, 2, d * S:(d + 1) * S],
                                                    Gh[:, d * 4 + s:d * 4 + s + 1], 0.0, ALU.add, ALU.min)
                    a.then_inc(arg_done, 1)

            def times_scores(h, par):
                sT = psum[:, 3:5, :].rearrange("p b (s t) -> p (b s) t", s=2)
                dve.wait_ge(sT_filled, h + 1)
                for d in range(2):
                    dve.wait_ge(w_exp, h * 2 + d + 1)
                    nc.vector.tensor_tensor(wts[par][:, d], wts[par][:, d], sT, ALU.mult).then_inc(w_mul, 1)

            def keep_squares(h):
                dve.wait_ge(h_sq, h * 2 + 3)
                nc.vector.tensor_copy(ssall[:, bass.ds(h, 1), :], ssh[:].unsqueeze(1)).then_inc(h_kept, 1)

            def head_out(h, par):
                nc.vector.tensor_copy(Eh[:].unsqueeze(2), Et[:, :, bass.ds(h, 1)]).then_inc(e_picked, 1)
                dve.wait_ge(h_filled, h + 2)
                sums_of = [psum[:, b, :].rearrange("p (t c) -> p t c", t=2) for b in ((5, 7)[par], 6)]
                nc.vector.tensor_copy(den[:, 0:2].unsqueeze(2), sums_of[0][:, :, MLV:MLV + 1])
                nc.vector.tensor_copy(den[:, 2:4].unsqueeze(2), sums_of[1][:, :, MLV:MLV + 1]).then_inc(h_step, 1)
                if not isinstance(h, int) or h > 0:
                    keep_squares(h - 1)
                dve.wait_ge(h_step, h * 7 + 1)
                nc.vector.tensor_scalar(dent[:], den[:], -1.0, None, ALU.mult).then_inc(h_step, 1)
                dve.wait_ge(h_step, h * 7 + 2)
                nc.vector.tensor_tensor(den[:], den[:], dent[:], ALU.max).then_inc(h_step, 1)
                dve.wait_ge(h_step, h * 7 + 3)
                dve.wait_ge(e_picked, h + 1)
                nc.vector.tensor_tensor(den[:], den[:], Eh[:], ALU.max).then_inc(h_step, 1)
                dve.wait_ge(h_step, h * 7 + 4)
                nc.vector.reciprocal(dent[:], den[:]).then_inc(h_step, 1)
                dve.wait_ge(h_step, h * 7 + 5)
                dve.wait_ge(h_sq, h * 2 + 1)
                H = L["H"]
                for t in range(2):
                    a = nc.vector.tensor_scalar(H[:, t, :], sums_of[0][:, t, 0:MLV], dent[:, t:t + 1], None, ALU.mult)
                a.then_inc(h_step, 1)
                dve.wait_ge(h_step, h * 7 + 6)
                for t in range(2):
                    a = nc.vector.scalar_tensor_tensor(out=H[:, t, :], in0=sums_of[1][:, t, 0:MLV],
                                                       scalar=dent[:, 2 + t:3 + t], in1=H[:, t, :], op0=ALU.mult,
                                                       op1=ALU.add)
                a.then_inc(h_ready, 1)
                dve.wait_ge(h_ready, h + 2)
                mo = kv["mo"][:, :, bass.ds(h * MLV, MLV)]
                nc.vector.tensor_tensor(mo, mo, H, ALU.mult).then_inc(h_step, 1)

            def head_step(h, par):
                exponents(h + 1, 1 - par)
                if not isinstance(h, int) or h < MLH - 2:
                    pick(h + 2)
                times_scores(h + 1, 1 - par)
                head_out(h, par)

            pick(0)
            exponents(0, 0)
            pick(1)
            times_scores(0, 0)
            heads(dve, head_step, 2)
            head_out(MLH - 1, 1)
            nc.vector.memset(place_of("y", D - W, W, 0, OUT), 0.0).then_inc(eps_set, 1)
            nc.vector.tensor_copy(scalev[:, :, 0], colsc[:, 0:KT]).then_inc(vec_ready, 1)
            dve.wait_ge(vec_ready, IN_VECS + 1)
            dve.wait_ge(eps_set, 5)
            for k in range(KT):
                turn(OUT, 0, 0, k, IN_TR + k, KT * NG + k, bank=k)
            for i in range(8):
                dve.wait_ge(pool_filled, i + 1)
                g, t = i // 2, i % 2
                dst = kv["z"][:, t, AT_POOL + g * PC:AT_POOL + (g + 1) * PC]
                nc.vector.tensor_tensor(dst, psum[:, i % 4, 0:PC], dst, ALU.mult).then_inc(pool_mixed, 1)
            keep_squares(MLH - 1)
            dve.wait_ge(ml_root, 1)
            nc.vector.reciprocal(rall[:], rall[:]).then_inc(ml_rstd, 1)
            dve.wait_ge(ml_rstd, 1)
            dve.wait_ge(h_step, 7 * MLH)
            groups(dve, OUT, group)

            n = OUT.n - 1
            dve.wait_ge(gate_kept, n + 1)
            dve.wait_ge(xe_in, 32)
            dve.wait_ge(added, IN_PAIRS + OUT.npairs * NG)
            gate = gate_rows[:, n * W:(n + 1) * W].unsqueeze(1).to_broadcast([P, 2, W])
            nc.vector.tensor_tensor(y_tile(n), y_tile(n), gate, ALU.mult).then_inc(last_step, 1)
            dve.wait_ge(last_step, 1)
            nc.vector.tensor_tensor(y_tile(n), y_tile(n), kv["z"][:, :, n * W:(n + 1) * W], ALU.add).then_inc(last_step, 1)
            dve.wait_ge(e_sq, 2 * OUT.n)
            nc.vector.tensor_reduce(sums[:, 0:2], rall[:].rearrange("p n t -> p t n"), AX_X, ALU.add).then_inc(e_rstd, 1)
            dve.wait_ge(e_root, 1)
            nc.vector.reciprocal(rstd[:, 0:2], rstd[:, 0:2]).then_inc(e_rstd, 1)
            dve.wait_ge(e_rstd, 2)
            for t in range(2):
                for n in range(Y_ACT, OUT.n):
                    y = y_tile(n)[:, t, :]
                    nc.vector.scalar_tensor_tensor(out=y, in0=y, scalar=rstd[:, t:t + 1], in1=fw[:, n * W:(n + 1) * W],
                                                   op0=ALU.mult, op1=ALU.mult).then_inc(dve_out, 1)

        @block.tensor
        def _(pe):
            def three(dst, left, right, first, last):
                passes = ((0, 0), (0, 1), (1, 0))
                for n, (a, b) in enumerate(passes):
                    m = nc.tensor.matmul(dst, left(a), right(b), start=first and n == 0, stop=last and n == 2)
                return m

            def mod_tile(kc, slot, landed_at, copied):
                pe.wait_ge(landed[IN][slot], landed_at)
                if kc == 0:
                    pe.wait_ge(mod_copied, copied)
                for q in range(KT):
                    m = nc.tensor.matmul(psum[32 * q:32 * q + 2, MOD_BANK, :], cT[:, :, KT * kc + q], raw[:, slot, q, :],
                                         start=kc == 0, stop=kc == 7)
                m.then_inc(mod_used, 1)

            def vec(use, copied):
                pe.wait_ge(mod_copied, copied)
                pe.wait_ge(tr_read, use)
                for k in range(KT):
                    m = nc.tensor.matmul(TR[:, 2 * k:2 * k + 2], modsb[:, k * P:(k + 1) * P], sel2, start=True, stop=True)
                m.then_inc(tr_filled, 1)

            def turn(pr, k, use, ready, bank=TR_BANK):
                pe.wait_ge(xs_ready, ready)
                if bank == TR_BANK:
                    pe.wait_ge(tr_read, use)
                for t in range(TT if pr is IN else 2):
                    m = nc.tensor.transpose(psum[:, bank, t * P:(t + 1) * P], xs[:, t, k * P:(k + 1) * P], ident)
                m.then_inc(tr_filled, 1)

            def column_tile(pr, j, g, buf, first):
                name, _, _, width = pr.tiles[j]
                q0, n = pr.pair[j]
                for i in range(n):
                    if (need := pr.pair_free(q0 + i, g, first)) is not None:
                        pe.wait_ge(added, need)
                for k in range(KT):
                    place = (KT * j + k) % PART
                    pe.wait_ge(lo_done, pr.chunk(j, k, g))
                    for i in range(n):
                        for t in range(2):
                            tok = slice((2 * i + t) * P, (2 * i + t + 1) * P)
                            m = three(psum[:, banks(q0 + i) + t, 0:width], lambda a: hT[:, buf, a, k, tok],
                                      lambda b: part[:, place, b, 0:width], k == 0, k == KT - 1)
                    m.then_inc(chunk_used, 1)

            def gate_tiles(i):
                if i == 0:
                    pe.wait_ge(gate_row, 1)
                    pe.wait_ge(tr_read, IN_TR + OUT.ntr * (NG - 1))
                else:
                    pe.wait_ge(gate_kept, 2 * i)
                for n in (2 * i, 2 * i + 1):
                    for k in range(KT):
                        m = nc.tensor.matmul(psum[:, MOD_BANK + n % 2, k * P:(k + 1) * P],
                                             ident[0:32, KT * n + k:KT * n + k + 1].to_broadcast([32, P]), gateR,
                                             start=True, stop=True)
                    m.then_inc(gate_filled, 1)

            def group(pr, g, buf, first, last):
                events, _, _ = turn_events(pr, last)
                pe.wait_ge(loT_done, g * KT + pr.hT0)
                for idx, item in enumerate(pr.order[last]):
                    if item[0] == "m":
                        kind = 0 if last else item[1]
                        mod_tile(item[2], pr.slot(idx), pr.landed_at(idx, g), g * 3 + (2 + kind))
                        continue
                    j = item[1]
                    column_tile(pr, j, g, buf, first)
                    if pr is OUT and last and j < 4:
                        gate_tiles(j)
                    for what, number, use in events.get(j, ()):
                        use = g * pr.ntr + (pr.tr0 + use)
                        if what == "vec":
                            kind = 0 if last else number
                            vec(use, g * 3 + (3 + kind))
                        else:
                            turn(pr, number, use, g * TT + 2 * TT if pr is IN else g + (TT * NG + 2))

            for s in (s_filled, p_turned, qr_turned, o_filled, ml_turned, h_filled):
                pe.sem_inc(s, 1)
            pe.wait_ge(par_in, 16 * PARAM_LOADS)
            for n, rows in enumerate((P, 96)):
                pe.wait_ge(tr_read, n)
                nc.tensor.transpose(TR[:, 0:rows], par_rows[0:rows, n, :], ident[0:rows, 0:rows]).then_inc(tr_filled, 1)
            pe.wait_ge(c_ready, 1)
            pe.wait_ge(mod_zero, 1)
            for n in range(PRO_MODS):
                mod_tile(n % 8, n % RAW, 16 * (n // RAW + 1), n // 8)
                if n == 8:
                    vec(2, 1)
            vec(3, 2)
            for k in range(KT):
                turn(IN, k, 4 + k, TT, bank=k)
            groups(pe, IN, group)

            pe.wait_ge(mod_copied, IN_VECS)
            pe.wait_ge(tr_read, IN_TR)
            pe.wait_ge(kr_roped, 4)
            for t in range(TT):
                m = nc.tensor.transpose(psum[:, 7, t * P:(t + 1) * P], key2[:, t].rearrange("p e c -> p (e c)"), ident)
            m.then_inc(kr_turned, 1)
            pe.wait_ge(cq_scaled, 6)
            pe.wait_ge(added, IN_PAIRS)
            for n in range(8):
                for i in range(4):
                    if n < 4:
                        src = kv["cq"][:, i % 2, (2 * n + i // 2) * P:(2 * n + i // 2 + 1) * P]
                    else:
                        src = kv["ckv"][:, i, (n - 4) * P:(n - 3) * P]
                    if n == 7 and i == 0:
                        pe.wait_ge(krT_ready, 1)
                    m = nc.tensor.transpose(psum[:, n, i * P:(i + 1) * P], src, ident)
                m.then_inc(lat_turned, 1)

            def cqT(a, kk, tok):
                at = (kk % 2) * S
                return hT[:, 0, a, kk // 2, at + tok.start:at + tok.stop]

            pe.wait_ge(lat_lo, 4)
            with pe.Fori(0, PAIRS) as hp:
                pe.wait_ge(p_ready, hp * 4 + 1)

                def rope_part(n):
                    w = part[:, n % PART]
                    for t in range(2):
                        m = three(psum[:, 2 + t, 0:2 * ROPE].rearrange("p (e c) -> p e c", e=2),
                                  lambda a: cqT(a, n, slice(t * P, (t + 1) * P)),
                                  lambda b: w[:, b, 0:384].rearrange("p (e c) -> p e c", e=2)[:, :, NOPE:192],
                                  n == 0, n == 7)
                    return m

                for n in range(PART):
                    pe.wait_ge(lo_done, hp * MLA_CHUNKS + (IN_CHUNKS + n + 1))
                    rope_part(n)
                pe.wait_ge(o_stored, hp * 4 + 1)
                for n in range(8):
                    pe.wait_ge(lo_done, hp * MLA_CHUNKS + (IN_CHUNKS + n + 1))
                    w = part[:, n % PART]
                    for e in range(2):
                        m = three(psum[:, e, 0:S], lambda b: w[:, b, e * 192:e * 192 + NOPE],
                                  lambda a: cqT(a, n, slice(0, S)), n == 0, n == 7)
                    if n >= PART:
                        m = rope_part(n)
                    m.then_inc(chunk_used, 1)
                for n in range(KT):
                    pe.wait_ge(lo_done, hp * MLA_CHUNKS + (IN_CHUNKS + 8 + n + 1))
                    w = part[:, n % PART]
                    if n == 0:
                        pe.wait_ge(lat_lo, 8)
                    for e in range(2):
                        m = three(psum[:, 4 + e, :], lambda b: w[:, b, e * 256:e * 256 + NOPE], lambda a: hT[:, 1, a, n, :],
                                  n == 0, n == KT - 1)
                    if n == KT - 1:
                        m.then_inc(kn_filled, 1)
                    for t in range(TT):
                        if n == 0 and t == 0:
                            pe.wait_ge(pT_ready, hp * 4 + 1)
                        if n == 0 and t == 2:
                            pe.wait_ge(qn_copied, hp + 1)
                        m = three(psum[:, (6, 7, 0, 1)[t], 0:2 * DV].rearrange("p (e c) -> p e c", e=2),
                                  lambda a: hT[:, 1, a, n, t * P:(t + 1) * P],
                                  lambda b: w[:, b, :].rearrange("p (e c) -> p e c", e=2)[:, :, NOPE:256],
                                  n == 0, n == KT - 1)
                    m.then_inc(chunk_used, 1)
                pe.wait_ge(q_roped, hp * 2 + 3)
                for t in range(2):
                    m = nc.tensor.transpose(psum[:, 2, t * P:(t + 1) * P], A["qr"][:, t].rearrange("p e c -> p (e c)"), ident)
                m.then_inc(qr_turned, 1)
                pe.wait_ge(kn_copied, hp + 1)

                def no_rope(i):
                    q = slice((i // 2) * P, (i // 2 + 1) * P)
                    nc.tensor.matmul(psum[:, 2 + i, :], A["qnT"][:, i % 2, q], A["knT"][:, i % 2, :], start=True, stop=False)

                no_rope(1)
                no_rope(2)
                no_rope(3)
                pe.wait_ge(qrT_copied, hp + 1)
                no_rope(0)
                for i in range(4):
                    q = slice((i // 2) * P, (i // 2 + 1) * P)
                    half = slice((i % 2) * ROPE, (i % 2 + 1) * ROPE)
                    nc.tensor.matmul(psum[:, 2 + i, :], A["qrT"][half, q], krT[half, :], start=False,
                                     stop=True).then_inc(s_filled, 1)

                def turn_probs(i):
                    pe.wait_ge(p_ready, hp * 4 + i + 2)
                    if i < 2:
                        pe.wait_ge(v_copied, hp * 2 + 1)
                    else:
                        pe.wait_ge(pT_ready, hp * 4 + i - 1 + 1)
                    for t in range(TT):
                        m = nc.tensor.transpose(psum[:, 6 + i % 2, t * P:(t + 1) * P], prob[:, i, t * P:(t + 1) * P], ident)
                    m.then_inc(p_turned, 1)

                def head_out(i):
                    pe.wait_ge(pT_ready, hp * 4 + i + 2)
                    if i < 2:
                        pe.wait_ge(v_copied, hp * 2 + 2)
                    else:
                        pe.wait_ge(o_stored, hp * 4 + i - 1 + 1)
                    for t in range(TT):
                        m = nc.tensor.matmul(psum[:, i % 2, 0:DV], probT[i % 2][:, t * P:(t + 1) * P],
                                             A["v"][:, t, (i % 2) * DV:(i % 2 + 1) * DV], start=t == 0, stop=t == TT - 1)
                    m.then_inc(o_filled, 1)

                turn_probs(0)
                turn_probs(1)
                head_out(0)
                turn_probs(2)
                head_out(1)
                turn_probs(3)
                head_out(2)
                head_out(3)

            pe.wait_ge(p_ready, 4 * PAIRS + 1)
            for n in range(4):
                for t in range(TT):
                    at = ((t + 2) % TT) * P
                    m = nc.tensor.transpose(psum[0:MLH, 2 + n, at:at + P], kv["kg"][:, t, 64 + n * MLH:64 + (n + 1) * MLH], ident)
            m.then_inc(g_turned, 1)
            pe.wait_ge(g_step, G_STEPS)
            id8 = ident[0:MLH, 0:MLH]
            for n in range(8):
                nc.tensor.transpose(psum[:, 4, n * MLH:(n + 1) * MLH], R["G"][0:MLH, n // 4, (n % 4) * P:(n % 4 + 1) * P], id8)
            for n in range(4):
                m = nc.tensor.transpose(psum[:, 4, 64 + n * MLH:64 + (n + 1) * MLH],
                                        R2["li"][0:MLH, n // 2, S + (n % 2) * P:S + (n % 2 + 1) * P], id8)
            m.then_inc(gt_turned, 1)
            pe.wait_ge(et_ready, 1)
            pe.wait_ge(gt_ready, 1)

            def turn_head(h):
                pe.wait_ge(staged, h * 2 + 4)
                pe.wait_ge(picked, h * 2 + 2)
                if not isinstance(h, int) or h > 0:
                    pe.wait_ge(ml_copied, h * 3 - 1)
                    pe.wait_ge(arg_done, h * 2)
                for s in range(4):
                    nc.tensor.transpose(psum[0:DQK, 0, s * P:(s + 1) * P], L["kst"][:, (s + 2) % 4, :], ident)
                for t in range(2):
                    nc.tensor.transpose(psum[0:DQK, 1, t * P:(t + 1) * P], L["qst"][:, t, :], ident)
                nc.tensor.matmul(psum[:, 2, :], selh[:], L["negM"][0:MLH].rearrange("p d t -> p (d t)"), start=True,
                                 stop=True).then_inc(ml_turned, 1)

            def scores(h):
                pe.wait_ge(ml_copied, h * 3 + 2)
                pe.wait_ge(w_mul, h * 2 + 1)
                for s in range(4):
                    m = nc.tensor.matmul(psum[:, 3 + s // 2, (s % 2) * S:(s % 2 + 1) * S], L["kT"][0:DQK, s * P:(s + 1) * P],
                                         L["qT"][0:DQK, :], start=True, stop=True)
                m.then_inc(sT_filled, 1)

            def values(h, par, d):
                pe.wait_ge(w_ready, h * 2 + d + 1)
                if d == 0:
                    pe.wait_ge(ml_copied, h * 3 + 3)
                    if not isinstance(h, int) or h > 1:
                        pe.wait_ge(h_ready, h)
                else:
                    pe.wait_ge(h_ready, h + 1)
                for t in range(2):
                    seen = [0, 1] + [2 + s for s in range(2) if (s <= t if d == 0 else s >= t)]
                    for s in seen:
                        m = nc.tensor.matmul(psum[:, (5, 7)[par] if d == 0 else 6, t * S:t * S + MLV + 1],
                                             wts[par][:, d, s, t * P:(t + 1) * P], vst[par][:, (s + 2) % 4, 0:MLV + 1],
                                             start=s == seen[0], stop=s == seen[-1])
                if d == 1:
                    m.then_inc(h_filled, 1)

            def head_step(h, par):
                turn_head(h + 1)
                values(h, par, 0)
                scores(h + 1)
                values(h, par, 1)

            turn_head(0)
            scores(0)
            heads(pe, head_step, 0)
            values(MLH - 1, 1, 0)
            values(MLH - 1, 1, 1)

            pe.wait_ge(arg_done, 2 * MLH)
            pe.wait_ge(w_mul, 2 * MLH + 1)
            for k in range(KT):
                turn(OUT, k, IN_TR + k, TT * NG + 1, bank=k)
            for slot in range(2):
                pe.wait_ge(landed[OUT][slot], 16)
            for i in range(8):
                g = i // 2
                if i in (1, 2):
                    pe.wait_ge(h_ready, MLH + i - 1)
                if i >= 4:
                    pe.wait_ge(pooled_copied, i - 3)
                for s in range(2):
                    m = nc.tensor.matmul(psum[:, 4 + i % 4, 0:S], kv["pu"][:, s, i * P:(i + 1) * P], band[:, s, g, :],
                                         start=s == 0, stop=s == 1)
                m.then_inc(pooled, 1)
            pe.wait_ge(loT_done, OUT.hT0)
            for i in range(8):
                g, t = i // 2, i % 2
                pe.wait_ge(pooled_copied, 2 * g + 2)
                if i >= 4:
                    pe.wait_ge(pool_mixed, i - 3)
                for cc in range(2):
                    m = nc.tensor.matmul(psum[:, i % 4, 0:PC], poolT[:, 2 * g + cc, t * P:(t + 1) * P], poolw[:, g, cc, :],
                                         start=cc == 0, stop=cc == 1)
                m.then_inc(pool_filled, 1)
            nc.tensor.transpose(psum[0:32, MOD_BANK, 0:P], gateK[:], ident).then_inc(gate_turned, 1)
            pe.wait_ge(pool_mixed, 8)
            groups(pe, OUT, group)


def shape_constants():
    f = np.float32
    rows, cols = np.repeat(np.arange(S // GRID_W), GRID_W), np.tile(np.arange(GRID_W), S // GRID_W)
    n = ROPE // 4
    inv = np.power(f(ROPE_BASE), -np.arange(n, dtype=f) / f(n)).astype(f)
    ang = np.concatenate([rows.astype(f)[:, None] * inv, cols.astype(f)[:, None] * inv], axis=1)
    halves = lambda a: np.concatenate([a[0:P], a[P:2 * P]], axis=1)
    pick = (np.arange(P)[:, None] % 32 == np.arange(2)[None, :]).astype(f)
    tables = np.concatenate([np.eye(P, dtype=f), halves(np.cos(ang)), halves(np.sin(ang)), pick], axis=1).astype(f)
    key, query = np.arange(P)[:, None], np.arange(P)[None, :]
    masks = np.concatenate([(key <= query).astype(f), (key >= query).astype(f)], axis=1)
    b = []
    key, query = np.arange(S)[:, None], np.arange(S)[None, :]
    for w in WINDOWS:
        lo, hi = np.clip(query - w // 2, 0, S), np.clip(query + w - w // 2, 0, S)
        mean = ((key >= lo) & (key < hi)).astype(np.float64) / (hi - lo)
        b.append((mean - (key == query)).astype(f))
    b = np.stack(b, axis=1)
    bands = np.stack([b[0:P], b[P:2 * P]], axis=1).reshape(P, -1)
    return {"tables": np.ascontiguousarray(tables), "masks": np.ascontiguousarray(masks),
            "bands": np.ascontiguousarray(bands)}


INS = ["x", "c", "ctx", "c_ctx", "norm_w", "w_mod", "b_mod", "w_in", "q_norm_w", "kv_norm_w", "w_uq", "w_ukv", "ml_b_i",
       "ml_b_f", "ml_norm_w", "pool_w", "pool_scale", "w_out", "final_norm_w"]


def kernel(**inputs):
    import concourse.bacc as bacc
    from concourse.bass_utils import run_bass_kernel_spmd

    nc = bacc.Bacc("TRN2", target_bir_lowering=False, num_devices=1)
    given = {name: np.ascontiguousarray(inputs[name]) for name in INS}
    given.update(shape_constants())
    arrays, args = {}, []
    for name, a in given.items():
        arrays[f"in_{name}"] = a
        args.append(nc.dram_tensor(f"in_{name}", a.shape, mybir.dt.from_np(a.dtype), kind="ExternalInput").ap())
    out = nc.dram_tensor("out_y", (1, S, D), F32, kind="ExternalOutput").ap()
    hybrid_kernel(nc, *args, out)
    r = run_bass_kernel_spmd(nc, [arrays], core_ids=[0])
    return r.results[0]["out_y"]
```
